# Optimizing a Trainium2 kernel written in Bass

```python
import jax, jax.numpy as jnp
from jax import lax
import numpy as np

D_MODEL = 1024
BATCH = 1
SEQ = 512
DEPTH = 1
DEC_BATCH = 8
DEC_SEQ = 4
PAST_LEN = 1024
PAGE_SIZE = 128

MIX_WIDTH = D_MODEL
N_HEADS = 8
HEAD_DIM = 64
N_KV_HEADS = 4
KV_GROUP = N_HEADS // N_KV_HEADS
ATT_WIDTH = N_HEADS * HEAD_DIM
KV_WIDTH = N_KV_HEADS * HEAD_DIM
MOBA_BLOCK = 256
MOBA_TOP_K = 3
Q_BLOCK = 32
GM_WIDTH = MIX_WIDTH - ATT_WIDTH
GM_GROUPS = 8
GM_GROUP_DIM = GM_WIDTH // GM_GROUPS
GM_CHUNK = 128
IN_COLS = ATT_WIDTH + 2 * KV_WIDTH + ATT_WIDTH + 3 * GM_WIDTH
NORM_EPS = 1e-6
LN_EPS = 1e-5

kernel_name = "hymba_moba_gmlp_decoder_step"

def rms_norm(x, g):
    xf = x.astype(jnp.float32)
    y = xf * lax.rsqrt(jnp.mean(xf * xf, axis=-1, keepdims=True) + NORM_EPS)
    return (y * g.astype(jnp.float32)).astype(x.dtype)

def group_layer_norm(v, g):
    shp = v.shape
    vf = v.astype(jnp.float32).reshape(shp[:-1] + (GM_GROUPS, GM_GROUP_DIM))
    mu = jnp.mean(vf, axis=-1, keepdims=True)
    var = jnp.mean(jnp.square(vf - mu), axis=-1, keepdims=True)
    y = ((vf - mu) * lax.rsqrt(var + LN_EPS)).reshape(shp)
    return (y * g.astype(jnp.float32)).astype(v.dtype)

def to_blocks(k):
    B, L = k.shape[:2]
    lp = -(-L // MOBA_BLOCK) * MOBA_BLOCK
    k = jnp.pad(k, ((0, 0), (0, lp - L), (0, 0), (0, 0)))
    return k.reshape(B, lp // MOBA_BLOCK, MOBA_BLOCK, N_KV_HEADS, HEAD_DIM).transpose(0, 3, 1, 2, 4)

def moba_queries(q, qpos, kb, vb, kmean, k_own, v_own, own_blk):
    B, KVH, G, Q, D = q.shape
    nb = kb.shape[2]
    n_sel = min(MOBA_TOP_K, nb)
    scale = D ** -0.5
    gate = jnp.einsum('bkgqd,bknd->bkgqn', q, kmean).astype(jnp.float32)
    gate = jnp.where(jnp.arange(nb) < own_blk, gate, -jnp.inf)
    _, idx = lax.top_k(gate, n_sel)
    valid = idx < own_blk
    b_ix = jnp.arange(B)[:, None, None, None, None]
    h_ix = jnp.arange(KVH)[None, :, None, None, None]
    k_sel = kb[b_ix, h_ix, idx]
    v_sel = vb[b_ix, h_ix, idx]
    s_sel = jnp.einsum('bkgqd,bkgqmnd->bkgqmn', q, k_sel).astype(jnp.float32) * scale
    s_sel = jnp.where(valid[..., None], s_sel, -jnp.inf).reshape(B, KVH, G, Q, n_sel * MOBA_BLOCK)
    s_own = jnp.einsum('bkgqd,bknd->bkgqn', q, k_own).astype(jnp.float32) * scale
    kpos = own_blk * MOBA_BLOCK + jnp.arange(MOBA_BLOCK)
    s_own = jnp.where(kpos[None, :] <= qpos[:, None], s_own, -jnp.inf)
    p = jax.nn.softmax(jnp.concatenate([s_sel, s_own], axis=-1), axis=-1)
    p_sel = p[..., :n_sel * MOBA_BLOCK].reshape(B, KVH, G, Q, n_sel, MOBA_BLOCK).astype(vb.dtype)
    p_own = p[..., n_sel * MOBA_BLOCK:].astype(vb.dtype)
    return (jnp.einsum('bkgqmn,bkgqmnd->bkgqd', p_sel, v_sel)
            + jnp.einsum('bkgqn,bknd->bkgqd', p_own, v_own))

def moba_prompt(q, k, v):
    B, S = q.shape[:2]
    kb, vb = to_blocks(k), to_blocks(v)
    kmean = jnp.mean(kb.astype(jnp.float32), axis=3)
    qh = q.reshape(B, S, N_KV_HEADS, KV_GROUP, HEAD_DIM).transpose(0, 2, 3, 1, 4)
    nq = S // Q_BLOCK
    qc = jnp.moveaxis(qh.reshape(B, N_KV_HEADS, KV_GROUP, nq, Q_BLOCK, HEAD_DIM), 3, 0)

    def step(args):
        qi, c = args
        start = c * Q_BLOCK
        qpos = start + jnp.arange(Q_BLOCK)
        own = start // MOBA_BLOCK
        k_own = lax.dynamic_index_in_dim(kb, own, axis=2, keepdims=False)
        v_own = lax.dynamic_index_in_dim(vb, own, axis=2, keepdims=False)
        return moba_queries(qi, qpos, kb, vb, kmean, k_own, v_own, own)

    out = lax.map(step, (qc, jnp.arange(nq, dtype=jnp.int32)))
    return out.transpose(1, 0, 4, 2, 3, 5).reshape(B, S, ATT_WIDTH)

def moba_sample(q, k_new, v_new, k_past, v_past):
    B, T = q.shape[:2]
    past_len = k_past.shape[1]
    kb = to_blocks(jnp.concatenate([k_past, k_new], axis=1))
    vb = to_blocks(jnp.concatenate([v_past, v_new], axis=1))
    kmean = jnp.mean(kb.astype(jnp.float32), axis=3)
    qh = q.reshape(B, T, N_KV_HEADS, KV_GROUP, HEAD_DIM).transpose(0, 2, 3, 1, 4)
    pos = past_len + jnp.arange(T)

    def one(qi, p):
        own = p // MOBA_BLOCK
        k_own = lax.dynamic_index_in_dim(kb, own, axis=2, keepdims=False)
        v_own = lax.dynamic_index_in_dim(vb, own, axis=2, keepdims=False)
        return moba_queries(qi[:, :, :, None], p[None], kb, vb, kmean, k_own, v_own, own)[:, :, :, 0]

    out = jax.vmap(one, in_axes=(3, 0), out_axes=3)(qh, pos)
    return out.transpose(0, 3, 1, 2, 4).reshape(B, T, ATT_WIDTH)

def gmlp_branch(u_raw, v_raw, g_sgu, w_sp, b_sp):
    B, L, _ = v_raw.shape
    u = jax.nn.gelu(u_raw)
    v = group_layer_norm(jax.nn.gelu(v_raw), g_sgu)
    lp = -(-L // GM_CHUNK) * GM_CHUNK
    up = jnp.pad(u, ((0, 0), (0, lp - L), (0, 0)))
    vp = jnp.pad(v, ((0, 0), (0, lp - L), (0, 0)))
    vc = vp.reshape(B, lp // GM_CHUNK, GM_CHUNK, GM_GROUPS, GM_GROUP_DIM)
    w = jnp.where(jnp.tril(jnp.ones((GM_CHUNK, GM_CHUNK), dtype=bool)), w_sp, 0)
    mixed = jnp.einsum('gts,bcsgd->bctgd', w, vc) + b_sp.T[:, :, None]
    out = up * mixed.reshape(B, lp, GM_WIDTH)
    return out[:, :L], v

def hybrid_layer(x, attend, g_pre, w_in, g_sgu, w_sp, b_sp, w_out, g_post):
    B, L, _ = x.shape
    h = rms_norm(x, g_pre)
    z = h @ w_in
    o1 = ATT_WIDTH
    o2 = o1 + KV_WIDTH
    o3 = o2 + KV_WIDTH
    o4 = o3 + ATT_WIDTH
    o5 = o4 + GM_WIDTH
    o6 = o5 + GM_WIDTH
    q, k, v, ga, u, vs, gg = jnp.split(z, [o1, o2, o3, o4, o5, o6], axis=-1)
    q = q.reshape(B, L, N_HEADS, HEAD_DIM)
    k = k.reshape(B, L, N_KV_HEADS, HEAD_DIM)
    v = v.reshape(B, L, N_KV_HEADS, HEAD_DIM)
    att = attend(q, k, v)
    gm, v_rows = gmlp_branch(u, vs, g_sgu, w_sp, b_sp)
    mix = jnp.concatenate([att * jax.nn.silu(ga), gm * jax.nn.silu(gg)], axis=-1)
    y = x + rms_norm(mix @ w_out, g_post)
    return y, k, v, v_rows

def setup_inputs(seed: int = 0) -> dict:
    key = jax.random.key(seed)
    ks = jax.random.split(key, 14)
    n_pages = PAST_LEN // PAGE_SIZE
    n_used = DEC_BATCH * n_pages
    n_phys = n_used + max(1, n_used // 4)
    nrm = jax.random.normal
    page_table = jax.random.permutation(ks[4], n_phys)[:n_used].reshape(DEC_BATCH, n_pages).astype(jnp.int32)
    return {
        "x_prompt": nrm(ks[0], (BATCH, SEQ, D_MODEL), jnp.float32),
        "x_sample": nrm(ks[1], (DEC_BATCH, DEC_SEQ, D_MODEL), jnp.float32),
        "cache_k": nrm(ks[2], (DEPTH, n_phys, PAGE_SIZE, N_KV_HEADS, HEAD_DIM), jnp.float32),
        "cache_v": nrm(ks[3], (DEPTH, n_phys, PAGE_SIZE, N_KV_HEADS, HEAD_DIM), jnp.float32),
        "page_table": page_table,
        "g_pre": 1.0 + 0.05 * nrm(ks[5], (DEPTH, D_MODEL), jnp.float32),
        "w_in": nrm(ks[6], (DEPTH, D_MODEL, IN_COLS), jnp.float32) * D_MODEL ** -0.5,
        "g_sgu": 1.0 + 0.05 * nrm(ks[7], (DEPTH, GM_WIDTH), jnp.float32),
        "w_spatial": nrm(ks[8], (DEPTH, GM_GROUPS, GM_CHUNK, GM_CHUNK), jnp.float32) * GM_CHUNK ** -0.5,
        "b_spatial": 1.0 + 0.1 * nrm(ks[9], (DEPTH, GM_GROUPS, GM_CHUNK), jnp.float32),
        "w_out": nrm(ks[10], (DEPTH, MIX_WIDTH, D_MODEL), jnp.float32) * MIX_WIDTH ** -0.5,
        "g_post": 1.0 + 0.05 * nrm(ks[11], (DEPTH, D_MODEL), jnp.float32),
    }

def reference(x_prompt, x_sample, cache_k, cache_v, page_table, g_pre, w_in, g_sgu,
              w_spatial, b_spatial, w_out, g_post):
    db, n_pages = page_table.shape
    past_len = n_pages * cache_k.shape[2]
    yp, ys = x_prompt, x_sample
    kp_l, vp_l, ks_l, vs_l, sv_l = [], [], [], [], []
    for l in range(DEPTH):
        yp, kp, vp, _ = hybrid_layer(yp, moba_prompt, g_pre[l], w_in[l], g_sgu[l],
                                     w_spatial[l], b_spatial[l], w_out[l], g_post[l])
        k_past = cache_k[l][page_table].reshape(db, past_len, N_KV_HEADS, HEAD_DIM)
        v_past = cache_v[l][page_table].reshape(db, past_len, N_KV_HEADS, HEAD_DIM)

        def attend_sample(q, k, v, k_past=k_past, v_past=v_past):
            return moba_sample(q, k, v, k_past, v_past)

        ys, kn, vn, sv = hybrid_layer(ys, attend_sample, g_pre[l], w_in[l], g_sgu[l],
                                      w_spatial[l], b_spatial[l], w_out[l], g_post[l])
        kp_l.append(kp)
        vp_l.append(vp)
        ks_l.append(kn)
        vs_l.append(vn)
        sv_l.append(sv)
    new_k_prompt = jnp.stack(kp_l)
    new_v_prompt = jnp.stack(vp_l)
    new_k_sample = jnp.stack(ks_l)
    new_v_sample = jnp.stack(vs_l)
    new_sgu_v_sample = jnp.stack(sv_l)
    return (yp, ys, new_k_prompt, new_v_prompt, new_k_sample, new_v_sample, new_sgu_v_sample)


_drawn_inputs = setup_inputs


def setup_inputs(seed=0):
    import zlib

    import numpy as np

    out = dict(_drawn_inputs(seed))
    spreads = {}
    factors = {}
    for name, (base, spread) in spreads.items():
        noise = np.random.default_rng([zlib.crc32(name.encode()), seed]).standard_normal(out[name].shape)
        drawn = base * np.exp(spread * noise) if base else spread * noise
        out[name] = __import__('jax').numpy.asarray(drawn.astype(out[name].dtype))
    for name, factor in factors.items():
        out[name] = (out[name] * factor).astype(out[name].dtype)
    return out
```

```python
from contextlib import ExitStack

import concourse.bass as bass
from concourse import mybir

fp32 = mybir.dt.float32
f32r = mybir.dt.float32r
bf16 = mybir.dt.bfloat16
i32 = mybir.dt.int32
ALU = mybir.AluOpType
ACT = mybir.ActivationFunctionType
AX = mybir.AxisListType

P = 128
D = 1024
KD = D // P
SEQ, DEC_B, DEC_T = 512, 8, 4
SMP = DEC_B * DEC_T
TOK = SEQ + SMP
HALF = TOK // 2
HEADS, KVH, HD = 8, 4, 64
KVW = KVH * HD
PAGE, PAGES = 128, 8
BLOCK = 256
NBLK = PAGE * PAGES // BLOCK
GRP, GCH = 8, 64
COLS = 3072
NEG = -1.0e30
RMS_EPS, LN_EPS = 1e-6, 1e-5
QSCALE = HD ** -0.5

Q_T, K_T, V_T, GA_T, U_T, VS_T, GG_T = 0, 4, 6, 8, 12, 16, 20
ORDER = ([("q", j, Q_T + j) for j in range(4)] + [("k", j, K_T + j) for j in range(2)]
         + [("v", j, V_T + j) for j in range(2)] + [("vs", j, VS_T + j) for j in range(4)]
         + [("u", j, U_T + j) for j in range(4)] + [("ga", j, GA_T + j) for j in range(4)]
         + [("gg", j, GG_T + j) for j in range(4)])
NT = len(ORDER)
TILE_OF = {(kind, j): n for n, (kind, j, _) in enumerate(ORDER)}
OUT_CHUNKS = [(hf, kp) for hf in range(2) for kp in (2, 3, 0, 1)]
NW = NT + len(OUT_CHUNKS)
TT = 5
ROWS = [P] * 4 + [SMP]
UNITS = [(kvh, i) for kvh in range(KVH) for i in range(4)]


def schedule():
    s = [("XT", 0), ("XT", 1), ("XT", 2), ("Z", 0, 0), ("XT", 3), ("XT", 4), ("Z", 0, 1)]
    side = {}

    def after(n, *steps):
        side.setdefault(n, []).extend(steps)

    after(4, ("WT",))
    for n, b in zip((6, 8, 10, 12), range(4)):
        after(n, ("KTR", 0, 0, b))
    after(16, ("KVN", 0), ("KVN", 1), ("DSC", 0, 0), ("DOWN", 0))
    after(17, ("KVN", 2), ("KVN", 3), ("KTR", 0, 1, 0))
    after(18, ("KVN", 4), ("KTR", 0, 1, 1))
    after(19, ("KTR", 0, 1, 2))
    after(20, ("KTR", 0, 1, 3))
    after(21, ("DSC", 0, 1), ("DSM", 0))
    after(22, ("KTR", 1, 0, 0))
    after(23, ("KTR", 1, 0, 1))
    after(24, ("KTR", 1, 0, 2), ("DPT", 0))
    after(25, ("KTR", 1, 0, 3), ("DPV", 0, 0))
    after(26, ("DSC", 1, 0), ("DPV", 0, 1), ("DOWN", 1))
    after(27, ("KTR", 1, 1, 0), ("KTR", 1, 1, 1), ("DOT", 0))
    after(28, ("KTR", 1, 1, 2), ("KTR", 1, 1, 3), ("VSN", 0))
    after(29, ("DSC", 1, 1), ("DSM", 1), ("VSN", 1))
    after(30, ("VSN", 2), ("VSN", 3))
    after(31, ("VSN", 4), ("DPT", 1), ("LN",))
    after(32, ("DPV", 1, 0))
    after(33, ("DPV", 1, 1))
    after(34, ("DOT", 1))
    n = 34
    for u in range(len(UNITS)):
        after(min(n, 47), ("PSC", u))
        if u >= 1:
            after(min(n, 47), ("PTR", u - 1))
        if u >= 2:
            after(min(n, 47), ("PPV", u - 2))
        after(min(n, 47), ("PN", u))
        n += 0 if u % 4 == 0 else 1
    for gp in range(3):
        after(2 * TILE_OF["gg", gp] + 3, ("SP", gp))
    for h in range(2, 2 * NT):
        s.append(("Z", h // 2, h % 2))
        s += side.get(h, [])
    s += [("PTR", 15), ("SP", 3), ("SPS",), ("PPV", 14)]
    s += [("MIX", 4), ("MIX", 5), ("PPV", 15), ("MIX", 6), ("MIX", 7), ("MIX", 0), ("MIX", 1), ("MIX", 2), ("MIX", 3)]
    s += [("Y", c) for c in range(len(OUT_CHUNKS))]
    return s


SCHEDULE = schedule()

T_OF, T_FREED_BY = {}, []
for _s in SCHEDULE:
    _by = {"XT": ["dve", "dve"], "KTR": ["act", "dve"], "WT": ["act", "act", "dve"], "KVN": ["act"],
           "DPT": ["act", "dve", "act"], "DOT": ["dve"], "VSN": ["dve"], "PTR": ["dve", "dve"],
           "SP": ["dve"], "SPS": ["dve"]}.get(_s[0], [])
    T_OF[_s] = len(T_FREED_BY)
    T_FREED_BY.extend(_by)


def freed(uses, n):
    return uses[n], sum(x == uses[n] for x in uses[:n + 1])


Z_FREED_BY = [{"q": "dve", "k": "dve", "v": "act", "vs": "act", "u": "act", "ga": "dve", "gg": "dve"}[kind]
              for kind, _, _ in ORDER for _ in range(2)]


HALF_BEFORE = {}
_h = -1
for _s in SCHEDULE:
    _h = 2 * _s[1] + _s[2] if _s[0] == "Z" else _h
    HALF_BEFORE[_s] = _h


def w_load_count(n):
    return sum(16 if 2 * m < NT else 32 for m in range(n // 2 % 2, n // 2 + 1, 2))


def position(kind):
    return {s: n for n, s in enumerate(s for s in SCHEDULE if s[0] == kind)}


KTR_N = position("KTR")
MIX_N = position("MIX")
KVN_N, VSN_N = position("KVN"), position("VSN")


def tokens(tt):
    return slice(tt * P, tt * P + ROWS[tt])


def build(nc, x_prompt, x_sample, cache_k, cache_v, page_table, g_pre, w_in, g_sgu, w_spatial,
          b_spatial, w_out, g_post, y_prompt, y_sample, k_prompt, v_prompt, k_sample, v_sample,
          sgu_sample):
    n_phys = cache_k.shape[1]
    x_src = [x_prompt[0, tokens(tt), :] for tt in range(4)] + [x_sample.rearrange("b t d -> (b t) d")]
    y_dst = [y_prompt[0, tokens(tt), :] for tt in range(4)] + [y_sample.rearrange("b t d -> (b t) d")]
    w_in_v = w_in[0].rearrange("(k p) c -> p k c", p=P)
    w_out_v = w_out[0].rearrange("(k p) c -> p k c", p=P)

    def kv_rows(prompt, sample, tt):
        if tt < 4:
            return prompt[0, 0, tokens(tt)].rearrange("s h d -> s (h d)")
        return sample[0].rearrange("b t h d -> (b t) (h d)")

    with ExitStack() as ctx:
        def sem(name):
            return ctx.enter_context(nc.semaphore(name))

        top = [-(-nc.sbuf_base // 32) * 32]

        def region(size):
            at = top[0]
            top[0] += size
            return at

        def place(name, shape, dt, at):
            return nc.alloc_sbuf_tensor_at(name, shape, dt, offset=at)

        R_H = region(2 * KD * TOK * 4)
        act_hi = place("act_hi", [P, KD, TOK], f32r, R_H)
        act_lo = place("act_lo", [P, KD, TOK], f32r, R_H + KD * TOK * 4)
        ZB = 4 * TOK * 4
        R_Z = region(3 * ZB)
        zu = place("zu", [P, 4, TOK], fp32, R_Z)
        zvs = place("zvs", [P, 4, TOK], fp32, R_Z + ZB)
        zga = place("zga", [P, 4, TOK], fp32, R_Z + ZB)
        kv32 = place("kv32", [P, 4, TOK], fp32, R_Z + 2 * ZB)
        zgg = place("zgg", [P, 4, TOK], fp32, R_Z + 2 * ZB)
        wsp = place("wsp", [P, GRP, P], fp32, R_Z + ZB)
        R_W = region(16384 + 16384)
        w_raw = place("w_raw", [P, 2, 2 * D], fp32, R_W)
        w_hi = place("w_hi", [P, 2, D], f32r, R_W + 16384)
        w_lo = place("w_lo", [P, 2, D], f32r, R_W + 24576)
        R_Q = region(32768)
        x_sb = place("x_sb", [P, TT, D], fp32, R_Q)
        xn = place("xn", [P, 2, D], fp32, R_Q + 20480)
        xg = place("xg", [P, 2, 512], fp32, R_Q + 28672)
        q_st = place("q_st", [P, HEADS, SEQ], f32r, R_Q)
        k_hi = place("k_hi", [P, KVH, SEQ], f32r, R_Q + 16384)
        k_lo = place("k_lo", [P, KVH, SEQ], f32r, R_Q + 24576)
        x_res = place("x_res", [P, TT, D], fp32, R_Q)
        R_V = region(4096 + 8192 + 10240)
        kvn = place("kvn", [P, 2, 512], fp32, R_V)
        ln_sq = place("ln_sq", [P, 512], fp32, R_V)
        g_sgu_bc = place("g_sgu_bc", [P, 512], fp32, R_V + 2048)
        v_st = place("v_st", [P, 4, KVH, 2 * HD], f32r, R_V + 4096)
        vn = place("vn", [P, TT, 512], fp32, R_V + 12288)
        qk_hi = place("qk_hi", [P, 2, SEQ], f32r, R_V + 12288)
        qk_lo = place("qk_lo", [P, 2, SEQ], f32r, R_V + 12288 + 4096)
        R_D = region(8192 + 16384 + 16384 + 4096 + 4096)
        k_ring = place("k_ring", [P, 2, 4, KVW], fp32, R_D)
        kT = place("kT", [P, 2, 4, 512], fp32, R_D + 8192)
        v_ring = place("v_ring", [P, 4, 4, KVW], fp32, R_D + 24576)
        pd = place("pd", [P, PAGE * PAGES], fp32, R_D + 40960)
        pdT = place("pdT", [P, PAGES, P], fp32, R_D + 45056)
        probs = place("probs", [P, 2, 2, SEQ], fp32, R_D)
        pT_hi = place("pT_hi", [P, 2, 4, 2, P], f32r, R_D + 8192)
        pT_lo = place("pT_lo", [P, 2, 4, 2, P], f32r, R_D + 16384)
        y_sb = place("y_sb", [P, TT, D], fp32, R_D)
        g_post_bc = place("g_post_bc", [P, D], fp32, R_D + 24576)
        b_bc = place("b_bc", [P, 4, P], fp32, R_D + 28672)
        th = place("th", [P, 2, HALF], fp32, R_D + 40960)
        att = place("att", [P, 2, P], fp32, R_D + 43136)
        o_tmp = place("o_tmp", [HD, 2, 256], fp32, R_D + 45056)
        sp_sum = place("sp_sum", [P, 512], fp32, R_D + 47104)
        R_C = region(0)

        def small(name, shape, dt=fp32):
            size = 1
            for d in shape[1:]:
                size *= d
            return place(name, shape, dt, region(-(-size * (2 if dt == bf16 else 4) // 32) * 32))

        ident = small("ident", [P, P])
        ident_h = small("ident_h", [P, P], bf16)
        causal = small("causal", [P, P], bf16)
        wspT = small("wspT", [P, GRP, P])
        g_pre_c = small("g_pre_c", [P, KD])
        own_mask = small("own_mask", [P, 2, SMP])
        bd_mask = small("bd_mask", [SMP, DEC_B, DEC_T])
        rep4 = small("rep4", [DEC_T, SMP])
        w_bd = small("w_bd", [SMP, GRP, SMP])
        pages_i = small("pages_i", [1, DEC_B * PAGES], i32)
        qbd = small("qbd", [P, 2, 2, P])
        q_s = small("q_s", [P, 4, SMP])
        att_s = q_s
        kv_s = small("kv_s", [SMP, 512])
        od = small("od", [P, KVW])
        p_own = small("p_own", [P, SMP])
        p_ownT = small("p_ownT", [SMP, P])
        own_s = small("own_s", [P, SMP])
        rank4 = small("rank4", [P, 4])
        stat = small("stat", [P, 64])
        ln_mu = small("ln_mu", [P, 2, GRP])
        ln_var = small("ln_var", [P, TT, GRP])
        ln_std = small("ln_std", [P, TT, GRP])
        ln_rstd = small("ln_rstd", [P, TT, GRP])
        nmax = small("nmax", [P, 2, 2])
        psums = small("psums", [P, 2, 2])
        rsum = small("rsum", [P, 2, 2])
        assert top[0] <= nc.sbuf_usable_end, (top[0], nc.sbuf_usable_end)
        x_ss, x_sd, x_rs = stat[:, 0:5], stat[:, 5:10], stat[:, 10:15]
        y_ss, y_sd, y_rs = stat[:, 15:25], stat[:, 25:30], stat[:, 30:35]
        gsum, bmax, wdrop, drop, bmsk, bbias = (stat[:, 35 + 4 * n:39 + 4 * n] for n in range(6))
        gmin, wmax, omax, tmax = (stat[:, 59 + n:60 + n] for n in range(4))
        dstat = small("dstat", [P, 16])
        nm_d, dsum, dtot, drec, y_sst = dstat[:, 0:1], dstat[:, 1:6], dstat[:, 6:7], dstat[:, 7:8], dstat[:, 8:13]
        assert top[0] <= nc.sbuf_usable_end, (top[0], nc.sbuf_usable_end)

        def psum(name, cols):
            return ctx.enter_context(nc.psum_tensor(name, [P, cols], fp32))

        Z = [psum("Z0", 512), psum("Z1", 512)]
        T = [psum("T0", 512), psum("T1", 512)]
        S = psum("S", 1024)
        O = [psum("O0", 512), psum("O1", 512)]
        Y = [[Z[0][:, :], Z[1][:, :], S[:, 0:512], S[:, 512:1024], T[0][:, :]],
             [O[0][:, :], O[1][:, :], Z[0][:, :], Z[1][:, :], T[1][:, :]]]

        x_in = [sem(f"x_in{t}") for t in range(TT)]
        xr_in = [sem(f"xr_in{t}") for t in range(TT)]
        consts_in = [sem(f"const_in{n}") for n in range(6)]
        gpre_in, wsp_in, b_in, gsgu_in, pages_in, gpost_in = consts_in
        w_in_s = [sem("w_in0"), sem("w_in1")]
        k_in = [sem("k_in0"), sem("k_in1")]
        v_in = [sem(f"v_in{n}") for n in range(4)]
        staged = [sem(f"staged{n}") for n in range(6)]
        stored_kv = [sem("stored_kv0"), sem("stored_kv1")]
        stored, stored_sgu = sem("stored"), sem("stored_sgu")
        consts_made = sem("consts_made")
        pool_step = sem("pool_step")
        wsp_masked = sem("wsp_masked")
        vn_done = sem("vn_done")
        ug_done = sem("ug_done")
        x_std = sem("x_std")
        x_hi = sem("x_hi")
        xn_done = sem("xn_done")
        xg_done = sem("xg_done")
        x_split = sem("x_split")
        w_hi_done = sem("w_hi_done")
        w_split = sem("w_split")
        z_full = sem("z_full")
        z_free = {"act": sem("z_free_act"), "dve": sem("z_free_dve")}
        t_full = sem("t_full")
        t_free = {"act": sem("t_free_act"), "dve": sem("t_free_dve")}
        z_hi = sem("z_hi")
        vst_hi, vst_done = sem("vst_hi"), sem("vst_done")
        rep_done, wbd_done = sem("rep_done"), sem("wbd_done")
        qbd_done = sem("qbd_done")
        dsc = sem("dsc")
        down = sem("down")
        d_bias = sem("d_bias")
        d_exp = sem("d_exp")
        d_rec = sem("d_rec")
        dpv = sem("dpv")
        od_done = sem("od_done")
        att_s_done = sem("att_s_done")
        psc = sem("psc")
        p_max = sem("p_max")
        p_exp = sem("p_exp")
        p_norm = sem("p_norm")
        pT_hi_done = sem("pT_hi_done")
        ppv = sem("ppv")
        o_hi = sem("o_hi")
        att_done = sem("att_done")
        sq_done, ssq_done, lnstd_done, lnmul_done = (sem(n) for n in ("sq_done", "ssq_done", "lnstd_done", "lnmul_done"))
        gm_done = sem("gm_done")
        mix_hi, mix_done = sem("mix_hi"), sem("mix_done")
        y_full = sem("y_full")
        y_out = sem("y_out")
        y_sq = sem("y_sq")
        y_ssq = sem("y_ssq")
        y_std = sem("y_std")
        y_done = sem("y_done")
        dve_chain = sem("dve_chain")
        act_chain = sem("act_chain")

        def bank_free(eng, n):
            if n >= 2:
                by, count = freed(T_FREED_BY, n - 2)
                eng.wait_ge(t_free[by], count)

        def z_bank_free(eng, h):
            if h >= 2:
                by, count = freed(Z_FREED_BY, h - 2)
                eng.wait_ge(z_free[by], count)

        def mix_ready(eng, k):
            eng.wait_ge(gm_done, 1)
            if k < KVH:
                eng.wait_ge(att_done, 4 * (k + 1))

        def w_slot_free(eng, n):
            if n - 2 >= NT:
                eng.wait_ge(y_full, TT * (n - 1 - NT))
            elif n >= 2:
                eng.wait_ge(z_full, 2 * (n - 1))

        def w_tile(n):
            return w_raw[:, n // 2 % 2, :].rearrange("p (k c) -> p k c", k=KD)[:, :, (n % 2) * P:(n % 2 + 1) * P] if n < NT \
                else w_raw[:, n // 2 % 2, (n % 2) * D:(n % 2 + 1) * D]

        def w_split_tile(w, n):
            return w[:, n % 2, :].rearrange("p (k c) -> p k c", k=KD) if n < NT else w[:, n % 2, :]

        block = ctx.enter_context(nc.Block())

        @block.sync
        def _(sp):
            sp.dma_start(pages_i[:, :], page_table.rearrange("(o b) p -> o (b p)", o=1)).then_inc(pages_in, 16)
            sp.dma_start(x_sb[:, 0, :], x_src[0]).then_inc(x_in[0], 16)
            sp.dma_start(g_pre_c[:, :], g_pre[0].rearrange("(k p) -> p k", p=P), allow_slow_non_contiguous=True).then_inc(gpre_in, 16)

            def load_w(m):
                if m >= 2:
                    sp.wait_ge(w_split, 2 * (m - 1))
                if 2 * m < NT:
                    col = ORDER[2 * m][2] * P
                    dst, src = w_raw[:, m % 2, :].rearrange("p (k c) -> p k c", k=KD), w_in_v[:, :, col:col + 2 * P]
                    sp.dma_start(dst, src).then_inc(w_in_s[m % 2], 16)
                else:
                    for e in range(2):
                        hf, kp = OUT_CHUNKS[2 * m - NT + e]
                        dst = w_raw[:, m % 2, e * D:(e + 1) * D].rearrange("p (k c) -> p k c", k=2)
                        sp.dma_start(dst, w_out_v[:, 2 * kp:2 * kp + 2, hf * 512:(hf + 1) * 512]).then_inc(w_in_s[m % 2], 16)

            def page(b, pg):
                at = b * PAGES + pg
                return sp.value_load(pages_i[0:1, at:at + 1], min_val=0, max_val=n_phys - 1)

            def load_k(m):
                r, kk, b = m // 8, m // 4 % 2, m % 4
                if m >= 2:
                    sp.wait_ge(t_full, T_OF["KTR", (m - 2) // 8, (m - 2) // 4 % 2, (m - 2) % 4] + 2)
                for j in range(4):
                    at = page(4 * r + b, 4 * kk + j)
                    sp.dma_start(k_ring[:, m % 2, j, :], cache_k[0, bass.ds(at, 1)].rearrange("a s h d -> (a s) (h d)"))\
                        .then_inc(k_in[m % 2], 16)

            def load_v(m):
                r, pg = m // PAGES, m % PAGES
                if m >= 4:
                    sp.wait_ge(dpv, m - 3)
                for b in range(4):
                    at = page(4 * r + b, pg)
                    sp.dma_start(v_ring[:, m % 4, b, :], cache_v[0, bass.ds(at, 1)].rearrange("a s h d -> (a s) (h d)"))\
                        .then_inc(v_in[m % 4], 16)

            for tt in (1, 2):
                sp.dma_start(x_sb[:, tt, :], x_src[tt]).then_inc(x_in[tt], 16)
            load_w(0)
            for tt in (3, 4):
                sp.dma_start(x_sb[0:ROWS[tt], tt, :], x_src[tt]).then_inc(x_in[tt], 16)
            load_w(1)
            sp.wait_ge(pages_in, 16)
            load_k(0)
            load_k(1)
            queue = []
            for m in range(2, NW // 2):
                queue.append((2 * (2 * m - 4) + 0.1, load_w, m))
            for m in range(2, 16):
                step = ("KTR", (m - 2) // 8, (m - 2) // 4 % 2, (m - 2) % 4)
                queue.append((HALF_BEFORE[step] + 0.5, load_k, m))
            for m in range(16):
                if m < 4:
                    queue.append((6 + m, load_v, m))
                else:
                    step = ("DPV", (m - 4) // 8, (m - 4) // 4 % 2)
                    queue.append((HALF_BEFORE[step] + 0.6, load_v, m))
            queue.sort(key=lambda q: q[0])
            rest_at = HALF_BEFORE["PSC", 15] + 0.7
            done_x = False
            for at, load, m in queue:
                if at > rest_at and not done_x:
                    done_x = True
                    sp.wait_ge(psc, len(UNITS))
                    for tt in range(TT):
                        sp.dma_start(x_res[0:ROWS[tt], tt, :], x_src[tt]).then_inc(xr_in[tt], 16)
                load(m)
            for tt in range(TT):
                sp.wait_ge(y_done, tt + 1)
                sp.dma_start(y_dst[tt], y_sb[0:ROWS[tt], tt, :]).then_inc(stored, 16)
            sp.wait_ge(stored, 16 * TT)
            sp.wait_ge(stored_sgu, 16)
            sp.wait_ge(stored_kv[0], 3 * 32)
            sp.wait_ge(stored_kv[1], 2 * 32)

        @block.gpsimd
        def _(pool):
            pool.dma_start(wsp[:, :, :], w_spatial[0].rearrange("g t s -> t g s")).then_inc(wsp_in, 16)

            count = [0]

            def link(ins):
                count[0] += 1
                ins.then_inc(pool_step, 1)
                pool.wait_ge(pool_step, count[0])

            nc.gpsimd.memset(ident[:, :], 0.0).then_inc(pool_step, 1)
            nc.gpsimd.memset(ident_h[:, :], 0.0).then_inc(pool_step, 1)
            nc.gpsimd.memset(causal[:, :], 0.0).then_inc(pool_step, 1)
            nc.gpsimd.memset(own_mask[:, :, :], 0.0).then_inc(pool_step, 1)
            nc.gpsimd.memset(bd_mask[:, :, :], 1.0).then_inc(pool_step, 1)
            count[0] = 5
            pool.wait_ge(pool_step, 5)

            def select(t, pattern, op, fill, base, mult):
                link(nc.gpsimd.affine_select(out=t, in_=t, pattern=pattern, compare_op=op, fill=fill,
                                             base=base, channel_multiplier=mult))

            select(ident[:, :], [[-1, P]], ALU.not_equal, 1.0, 0, 1)
            nc.gpsimd.memset(rank4[:, 0:1], 1.0).then_inc(consts_made, 1)
            select(ident_h[:, :], [[-1, P]], ALU.not_equal, 1.0, 0, 1)
            select(causal[:, :], [[-1, P]], ALU.is_ge, NEG, 0, 1)
            for r in range(2):
                m = own_mask[:, r, :].rearrange("p (b t) -> p b t", t=DEC_T)
                select(m, [[-32, DEC_B], [-8, DEC_T]], ALU.is_ge, NEG, 128 * r, 1)
                select(m, [[32, DEC_B], [0, DEC_T]], ALU.is_ge, NEG, 31 - 128 * r, -1)
            select(bd_mask[:, :, :], [[-4, DEC_B], [0, DEC_T]], ALU.is_ge, 0.0, 0, 1)
            select(bd_mask[:, :, :], [[4, DEC_B], [0, DEC_T]], ALU.is_ge, 0.0, 3, -1)
            for n in range(1, 4):
                nc.gpsimd.memset(rank4[:, n:n + 1], float(n + 1))
            nc.gpsimd.memset(qbd[:, :, :, :], 0.0).then_inc(consts_made, 1)
            pool.wait_ge(wsp_in, 16)
            nc.gpsimd.affine_select(out=wsp[:, :, :], in_=wsp[:, :, :], pattern=[[0, GRP], [-1, P]],
                                    compare_op=ALU.is_ge, fill=0.0, base=0, channel_multiplier=1)\
                .then_inc(wsp_masked, 1)

            for s in SCHEDULE:
                kind = s[0]
                if kind == "Z" and ORDER[s[1]][0] in ("q", "k") and s[2] == 1:
                    n = s[1]
                    what, j, _ = ORDER[n]
                    pool.wait_ge(z_free["dve"], freed(Z_FREED_BY, 2 * n + 1)[1])
                    for e in range(2):
                        rows, of = slice(e * HD, (e + 1) * HD), slice(0, HD)
                        lo_rows = slice(HD, P)
                        if what == "q":
                            pool.dma_start(q_st[of, 2 * j + e, :], qk_hi[rows, n % 2, :]).then_inc(staged[n], 16)
                            pool.dma_start(q_st[lo_rows, 2 * j + e, :], qk_lo[rows, n % 2, :]).then_inc(staged[n], 16)
                        else:
                            for half in (of, lo_rows):
                                pool.dma_start(k_hi[half, 2 * j + e, :], qk_hi[rows, n % 2, :]).then_inc(staged[n], 16)
                                pool.dma_start(k_lo[half, 2 * j + e, :], qk_lo[rows, n % 2, :]).then_inc(staged[n], 16)
                elif kind == "KVN":
                    tt = s[1]
                    src = kvn[:, tt % 2, :] if tt < 4 else kv_s[:, :]
                    pool.wait_ge(t_free["act"], freed(T_FREED_BY, T_OF[s])[1])
                    pool.dma_start(kv_rows(k_prompt, k_sample, tt), src[:, 0:KVW]).then_inc(stored_kv[tt % 2], 16)
                    pool.dma_start(kv_rows(v_prompt, v_sample, tt), src[:, KVW:2 * KVW]).then_inc(stored_kv[tt % 2], 16)
                elif kind == "Z" and s[1:] == (TILE_OF["vs", 2], 0):
                    pool.wait_ge(vst_done, 4)
                    pool.wait_ge(stored_kv[1], 2 * 32)
                    pool.dma_start(g_sgu_bc[:, :], g_sgu[0:1, :].broadcast_to([P, 512])).then_inc(gsgu_in, 16)
                elif kind == "PSC" and s[1] == 0:
                    pool.wait_ge(dpv, 2 * PAGES)
                    for e in range(2):
                        pool.dma_start(b_bc[e * HD:(e + 1) * HD, :, :],
                                       b_spatial[0].rearrange("(o g e) t -> e o g t", e=2, o=1)[e].broadcast_to([HD, 4, P])).then_inc(b_in, 16)
                    pool.dma_start(g_post_bc[:, :], g_post[0:1, :].broadcast_to([P, D])).then_inc(gpost_in, 16)
                elif kind == "LN":
                    pool.wait_ge(gsgu_in, 16)
                    for n, tt in enumerate((4, 0, 1, 2, 3)):
                        R = ROWS[tt]
                        pool.wait_ge(lnmul_done, n + 1)
                        nc.gpsimd.tensor_tensor(vn[0:R, tt, :], vn[0:R, tt, :], g_sgu_bc[0:R, :], ALU.mult).then_inc(vn_done, 1)
                        if tt == 4:
                            pool.wait_ge(vn_done, 1)
                            pool.dma_start(sgu_sample[0].rearrange("b t c -> (b t) c"), vn[0:SMP, 4, :]).then_inc(stored_sgu, 16)
                elif kind == "Z" and ORDER[s[1]][0] == "gg" and s[2] == 1:
                    j = ORDER[s[1]][1]
                    pool.wait_ge(z_free["dve"], freed(Z_FREED_BY, 2 * s[1] + 1)[1])
                    pool.wait_ge(z_free["act"], freed(Z_FREED_BY, 2 * TILE_OF["u", j] + 1)[1])
                    nc.gpsimd.tensor_tensor(zu[:, j, :], zu[:, j, :], zgg[:, j, :], ALU.mult).then_inc(ug_done, 1)

        @block.scalar
        def _(act):
            chain = [0]

            def link(ins):
                chain[0] += 1
                ins.then_inc(act_chain, 1)
                act.wait_ge(act_chain, chain[0])

            def split_hi(n):
                w_slot_free(act, n)
                act.wait_ge(w_in_s[n // 2 % 2], w_load_count(n))
                nc.scalar.activation(w_split_tile(w_hi, n), w_tile(n), ACT.Copy).then_inc(w_hi_done, 1)

            def x_stats(tt):
                R = ROWS[tt]
                act.wait_ge(x_in[tt], 16)
                if tt >= 2:
                    act.wait_ge(t_full, T_OF["XT", tt - 2] + 2)
                link(nc.scalar.activation(xn[0:R, tt % 2, :], x_sb[0:R, tt, :], ACT.Square, accum_out=x_ss[0:R, tt:tt + 1]))
                nc.scalar.activation(x_sd[0:R, tt:tt + 1], x_ss[0:R, tt:tt + 1], ACT.Sqrt, scale=1.0 / D, bias=RMS_EPS).then_inc(x_std, 1)

            hi_count = [0]

            def take(n, dst, src, free=True):
                act.wait_ge(t_full, n + 1)
                nc.scalar.activation(dst, src, ACT.Copy).then_inc(t_free["act"], 1)

            for s in SCHEDULE:
                kind = s[0]
                if kind == "XT":
                    tt = s[1]
                    if tt == 0:
                        x_stats(0)
                        x_stats(1)
                    for kk in range(2):
                        act.wait_ge(xg_done, 2 * tt + kk + 1)
                        R = ROWS[tt]
                        src = xg[:, kk, 0:4 * R].rearrange("p (k t) -> p k t", k=4)
                        nc.scalar.activation(act_hi[:, 4 * kk:4 * kk + 4, tokens(tt)], src, ACT.Copy).then_inc(x_hi, 1)
                    if tt == 0:
                        split_hi(0)
                    if tt + 2 < TT:
                        x_stats(tt + 2)
                    if tt == 2:
                        split_hi(1)
                elif kind == "Z":
                    n, half = s[1], s[2]
                    h = 2 * n + half
                    what, j, _ = ORDER[n]
                    if half == 0 and 2 <= n + 1 < NW:
                        split_hi(n + 1)
                    bank, cols = Z[h % 2], slice(half * HALF, (half + 1) * HALF)
                    act.wait_ge(z_full, h + 1)
                    if what in ("q", "k"):
                        np_ = HALF if half == 0 else SEQ - HALF
                        if n >= 2:
                            act.wait_ge(staged[n - 2], 64 if n - 2 < 4 else 128)
                        if what == "k":
                            link(nc.scalar.activation(kv32[:, j, cols], bank[:, 0:HALF], ACT.Copy))
                        elif half == 1:
                            link(nc.scalar.activation(q_s[:, j, :], bank[:, np_:HALF], ACT.Copy, scale=QSCALE))
                        nc.scalar.activation(qk_hi[:, n % 2, half * HALF:half * HALF + np_], bank[:, 0:np_], ACT.Copy,
                                             scale=QSCALE if what == "q" else 1.0).then_inc(z_hi, 1)
                    elif what == "v":
                        nc.scalar.activation(kv32[:, 2 + j, cols], bank[:, 0:HALF], ACT.Copy).then_inc(z_free["act"], 1)
                    elif what == "vs":
                        if n == TILE_OF["vs", 0] and half == 0:
                            act.wait_ge(t_full, T_OF["WT",] + 2)
                        nc.scalar.activation(zvs[:, j, cols], bank[:, 0:HALF], ACT.Gelu_apprx_tanh).then_inc(z_free["act"], 1)
                    elif what == "u":
                        nc.scalar.activation(zu[:, j, cols], bank[:, 0:HALF], ACT.Gelu_apprx_tanh).then_inc(z_free["act"], 1)
                    else:
                        g = h - 2 * TILE_OF["ga", 0]
                        if g >= 2:
                            act.wait_ge(z_free["dve"], freed(Z_FREED_BY, h - 2)[1])
                        nc.scalar.activation(th[:, g % 2, :], bank[:, 0:HALF], ACT.Tanh, scale=0.5).then_inc(z_hi, 1)
                elif kind == "WT":
                    n = T_OF[s]
                    for e in range(2):
                        take(n + e, wspT[:, 4 * e:4 * e + 4, :], T[(n + e) % 2][:, :].rearrange("p (g t) -> p g t", g=4))
                elif kind == "KVN":
                    n, tt = T_OF[s], s[1]
                    R = ROWS[tt]
                    if 2 <= tt < 4:
                        act.wait_ge(stored_kv[tt % 2], 32)
                        act.wait_ge(vst_done, tt - 1)
                    take(n, (kvn[:, tt % 2, :] if tt < 4 else kv_s[:, :]), T[n % 2][0:R, :])
                    if tt < 4:
                        act.wait_ge(t_free["act"], freed(T_FREED_BY, n)[1])
                        nc.scalar.activation(v_st[:, tt, :, 0:HD], kvn[:, tt % 2, KVW:].rearrange("p (h d) -> p h d", h=KVH), ACT.Copy)\
                            .then_inc(vst_hi, 1)
                elif kind == "KTR":
                    _, r, kk, b = s
                    n = T_OF[s]
                    if b == 0 and 2 * r + kk >= 1:
                        act.wait_ge(dsc, 2 * r + kk)
                    take(n, kT[:, 0, b, :], T[n % 2][:, :])
                elif kind == "DSM":
                    r = s[1]
                    act.wait_ge(d_bias, r + 1)
                    if r:
                        act.wait_ge(t_full, T_OF["DPT", r - 1] + 3)
                        act.wait_ge(d_rec, r)
                    for blk in range(NBLK):
                        cs = slice(blk * BLOCK, (blk + 1) * BLOCK)
                        nc.scalar.activation(pd[:, cs], S[:, cs], ACT.Exp, bias=bbias[:, blk:blk + 1],
                                             accum_out=dsum[:, blk:blk + 1]).then_inc(act_chain, 1)
                        chain[0] += 1
                    nc.scalar.activation(p_own[:, :], own_s[:, :], ACT.Exp, bias=nm_d, accum_out=dsum[:, 4:5]).then_inc(d_exp, 1)
                elif kind == "DPT":
                    r, n = s[1], T_OF[s]
                    if r:
                        act.wait_ge(dpv, PAGES * r)
                    take(n, pdT[:, 0:4, :], T[n % 2][:, :].rearrange("p (j q) -> p j q", j=4))
                    take(n + 2, p_ownT[:, :], T[(n + 2) % 2][0:SMP, 0:P])
                elif kind == "VSN":
                    tt = s[1]
                    R = ROWS[tt]
                    act.wait_ge(t_free["dve"], freed(T_FREED_BY, T_OF[s])[1])
                    if tt:
                        act.wait_ge(ssq_done, tt)
                    else:
                        act.wait_ge(stored_kv[0], 3 * 32)
                    nc.scalar.activation(ln_sq[0:R, :], vn[0:R, tt, :], ACT.Square).then_inc(sq_done, 1)
                elif kind == "LN":
                    act.wait_ge(ssq_done, TT)
                    nc.scalar.activation(ln_std[:, 0:4, :], ln_var[:, 0:4, :], ACT.Sqrt, scale=1.0 / GCH, bias=LN_EPS).then_inc(lnstd_done, 1)
                    nc.scalar.activation(ln_std[0:SMP, 4, :], ln_var[0:SMP, 4, :], ACT.Sqrt, scale=1.0 / GCH, bias=LN_EPS).then_inc(lnstd_done, 1)
                elif kind == "PSC":
                    u = s[1]
                    keys = P * (UNITS[u][1] + 1)
                    act.wait_ge(p_max, u + 1)
                    if u == 0:
                        act.wait_ge(dpv, 2 * PAGES)
                    if u >= 2:
                        act.wait_ge(t_full, T_OF["PTR", u - 2] + 2)
                        act.wait_ge(p_norm, 2 * u - 2)
                    for g in range(2):
                        ins = nc.scalar.activation(probs[:, u % 2, g, 0:keys], S[:, g * 512:g * 512 + keys], ACT.Exp,
                                                   bias=nmax[:, u % 2, g:g + 1], accum_out=psums[:, u % 2, g:g + 1])
                        ins.then_inc(p_exp, 1)
                elif kind == "PTR":
                    u, n = s[1], T_OF[s]
                    blocks = UNITS[u][1] + 1
                    if u == 0:
                        act.wait_ge(dsc, 4)
                    if u >= 2:
                        act.wait_ge(ppv, u - 1)
                    for g in range(2):
                        act.wait_ge(t_full, n + g + 1)
                        nc.scalar.activation(pT_hi[:, u % 2, 0:blocks, g, :],
                                             T[(n + g) % 2][:, 0:blocks * P].rearrange("p (j q) -> p j q", q=P), ACT.Copy)\
                            .then_inc(pT_hi_done, 1)
                elif kind == "PPV":
                    u = s[1]
                    act.wait_ge(ppv, u + 1)
                    if u >= 2:
                        act.wait_ge(att_done, u - 1)
                    nc.scalar.activation(o_tmp[:, u % 2, :], O[u % 2][HD:P, 0:256], ACT.Copy).then_inc(o_hi, 1)
                elif kind == "MIX":
                    k = s[1]
                    mix_ready(act, k)
                    act.wait_ge(z_full, 2 * NT)
                    nc.scalar.activation(act_hi[:, k, :], zga[:, k, :] if k < 4 else zgg[:, k - 4, :], ACT.Copy).then_inc(mix_hi, 1)
                elif kind == "Y":
                    c = s[1]
                    if NT + c + 1 < NW:
                        split_hi(NT + c + 1)
                    hf = OUT_CHUNKS[c][0]
                    if c % 4 == 3:
                        for tt in range(TT):
                            R = ROWS[tt]
                            act.wait_ge(y_out, TT * hf + tt + 1)
                            nc.scalar.activation(ln_sq[0:R, :], y_sb[0:R, tt, hf * 512:(hf + 1) * 512], ACT.Square,
                                                 accum_out=y_ss[0:R, 5 * hf + tt:5 * hf + tt + 1]).then_inc(y_sq, 1)
                            act.wait_ge(y_sq, TT * hf + tt + 1)
                            if hf == 1:
                                act.wait_ge(y_ssq, tt + 1)
                                nc.scalar.activation(y_sd[0:R, tt:tt + 1], y_sst[0:R, tt:tt + 1], ACT.Sqrt, scale=1.0 / D, bias=RMS_EPS)\
                                    .then_inc(y_std, 1)

        @block.vector
        def _(dve):
            chain = [0]

            def link(ins):
                chain[0] += 1
                ins.then_inc(dve_chain, 1)
                dve.wait_ge(dve_chain, chain[0])

            def split_lo(n):
                dve.wait_ge(w_hi_done, n + 1)
                nc.vector.tensor_tensor(w_split_tile(w_lo, n), w_tile(n), w_split_tile(w_hi, n).bitcast(fp32), ALU.subtract)\
                    .then_inc(w_split, 1)

            def x_norm(tt):
                R = ROWS[tt]
                dve.wait_ge(x_std, tt + 1)
                link(nc.vector.reciprocal(x_rs[0:R, tt:tt + 1], x_sd[0:R, tt:tt + 1]))
                nc.vector.tensor_scalar(xn[0:R, tt % 2, :], x_sb[0:R, tt, :], x_rs[0:R, tt:tt + 1], None, ALU.mult).then_inc(xn_done, 1)

            for s in SCHEDULE:
                kind = s[0]
                if kind == "XT":
                    tt, n = s[1], T_OF[s]
                    R = ROWS[tt]
                    if tt == 0:
                        x_norm(0)
                        x_norm(1)
                        dve.wait_ge(gpre_in, 16)
                    for kk in range(2):
                        dve.wait_ge(t_full, n + kk + 1)
                        dst = xg[:, kk, 0:4 * R].rearrange("p (k t) -> p k t", k=4)
                        nc.vector.tensor_tensor(dst, T[(n + kk) % 2][:, 0:4 * R].rearrange("p (k t) -> p k t", k=4),
                                                g_pre_c[:, 4 * kk:4 * kk + 4].unsqueeze(2).broadcast_to([P, 4, R]), ALU.mult)\
                            .then_inc(xg_done, 1)
                    for kk in range(2):
                        dve.wait_ge(x_hi, 2 * tt + kk + 1)
                        src = xg[:, kk, 0:4 * R].rearrange("p (k t) -> p k t", k=4)
                        nc.vector.tensor_tensor(act_lo[:, 4 * kk:4 * kk + 4, tokens(tt)], src,
                                                act_hi[:, 4 * kk:4 * kk + 4, tokens(tt)].bitcast(fp32), ALU.subtract)\
                            .then_inc(t_free["dve"], 1)
                    if tt == 0:
                        split_lo(0)
                    if tt + 2 < TT:
                        x_norm(tt + 2)
                    if tt == 2:
                        split_lo(1)
                elif kind == "Z":
                    n, half = s[1], s[2]
                    h = 2 * n + half
                    what, j, _ = ORDER[n]
                    bank, cols = Z[h % 2], slice(half * HALF, (half + 1) * HALF)
                    if what in ("q", "k"):
                        np_ = HALF if half == 0 else SEQ - HALF
                        cs = slice(half * HALF, half * HALF + np_)
                        dve.wait_ge(z_hi, h + 1)
                        ins = nc.vector.scalar_tensor_tensor(qk_lo[:, n % 2, cs], bank[:, 0:np_], QSCALE if what == "q" else 1.0,
                                                             qk_hi[:, n % 2, cs].bitcast(fp32), ALU.mult, ALU.subtract)
                        ins.then_inc(z_free["dve"], 1)
                        if n == 3 and half == 1:
                            dve.wait_ge(consts_made, 2)
                            view = qbd[:, :, :, :].rearrange("p c r (x h) -> p c r x h", h=HEADS)
                            for hd in range(HEADS):
                                kvh, g = hd // 2, hd % 2
                                to = (kvh % 2) * HD
                                ins = nc.vector.tensor_copy(view[to:to + HD, kvh // 2, :, :, hd],
                                                            q_s[g * HD:(g + 1) * HD, kvh, :].rearrange("p (r x) -> p r x", r=2))
                            ins.then_inc(qbd_done, 1)
                    elif what in ("ga", "gg"):
                        g = h - 2 * TILE_OF["ga", 0]
                        dst = zga if what == "ga" else zgg
                        dve.wait_ge(z_hi, 12 + g + 1)
                        if g == 0:
                            dve.wait_ge(t_full, T_OF["VSN", 4] + 1)
                        if what == "gg" and j == 0 and half == 0:
                            dve.wait_ge(t_full, T_OF["KVN", 4] + 1)
                            dve.wait_ge(down, 2)
                        nc.vector.scalar_tensor_tensor(dst[:, j, cols], th[:, g % 2, :], 1.0, bank[:, 0:HALF], ALU.add, ALU.mult)\
                            .then_inc(z_free["dve"], 1)
                    if half == 0 and 2 <= n + 1 < NW:
                        split_lo(n + 1)
                elif kind == "WT":
                    n = T_OF[s]
                    dve.wait_ge(consts_made, 2)
                    nc.vector.tensor_copy(rep4[:, :].rearrange("p (b t) -> p b t", t=DEC_T),
                                          ident[0:DEC_T, 0:DEC_T].unsqueeze(1).broadcast_to([DEC_T, DEC_B, DEC_T])).then_inc(rep_done, 1)
                    dve.wait_ge(t_full, n + 3)
                    nc.vector.tensor_tensor(w_bd[:, :, :].rearrange("p g (b t) -> p g b t", t=DEC_T),
                                            T[(n + 2) % 2][0:SMP, 0:GRP * DEC_T].rearrange("p (g t) -> p g t", g=GRP).unsqueeze(2).broadcast_to([SMP, GRP, DEC_B, DEC_T]),
                                            bd_mask[:, :, :].unsqueeze(1).broadcast_to([SMP, GRP, DEC_B, DEC_T]), ALU.mult)\
                        .then_inc(t_free["dve"], 1)
                elif kind == "KVN":
                    tt = s[1]
                    if tt < 4:
                        dve.wait_ge(vst_hi, tt + 1)
                        nc.vector.tensor_tensor(v_st[:, tt, :, HD:], kvn[:, tt % 2, KVW:].rearrange("p (h d) -> p h d", h=KVH),
                                                v_st[:, tt, :, 0:HD].bitcast(fp32), ALU.subtract).then_inc(vst_done, 1)
                elif kind == "KTR":
                    _, r, kk, b = s
                    n = T_OF[s] + 1
                    if b == 0 and 2 * r + kk >= 1:
                        dve.wait_ge(dsc, 2 * r + kk)
                    dve.wait_ge(t_full, n + 1)
                    nc.vector.tensor_copy(kT[:, 1, b, :], T[n % 2][:, :]).then_inc(t_free["dve"], 1)
                elif kind == "DOWN":
                    r = s[1]
                    dve.wait_ge(down, r + 1)
                    if r:
                        dve.wait_ge(d_exp, r)
                    link(nc.vector.tensor_tensor(own_s[:, :], O[0][:, 0:SMP], own_mask[:, r, :], ALU.add))
                elif kind == "DSM":
                    r = s[1]
                    dve.wait_ge(dsc, 2 * r + 2)
                    if r:
                        dve.wait_ge(d_exp, r)
                    blocks = S[:, :].rearrange("p (n c) -> p n c", n=NBLK)
                    nc.vector.tensor_reduce(gsum, blocks, AX.X, ALU.add).then_inc(dve_chain, 1)
                    nc.vector.tensor_reduce(bmax, blocks, AX.X, ALU.max).then_inc(dve_chain, 1)
                    chain[0] += 2
                    link(nc.vector.tensor_reduce(omax, own_s[:, :], AX.X, ALU.max))
                    link(nc.vector.tensor_reduce(gmin, gsum, AX.X, ALU.min))
                    link(nc.vector.scalar_tensor_tensor(wdrop, gsum, gmin, rank4[:, :], ALU.is_equal, ALU.mult))
                    link(nc.vector.tensor_reduce(wmax, wdrop, AX.X, ALU.max))
                    link(nc.vector.tensor_scalar(drop, wdrop, wmax, NEG, ALU.is_equal, ALU.mult))
                    link(nc.vector.tensor_tensor(bmsk, bmax, drop, ALU.add))
                    link(nc.vector.tensor_reduce(tmax, bmsk, AX.X, ALU.max))
                    link(nc.vector.tensor_scalar(nm_d, tmax, omax, -1.0, ALU.max, ALU.mult))
                    nc.vector.tensor_scalar(bbias, drop, nm_d, None, ALU.add).then_inc(d_bias, 1)
                    dve.wait_ge(d_exp, r + 1)
                    link(nc.vector.tensor_reduce(dtot, dsum, AX.X, ALU.add))
                    nc.vector.reciprocal(drec, dtot).then_inc(d_rec, 1)
                elif kind == "DPT":
                    n = T_OF[s] + 1
                    if s[1]:
                        dve.wait_ge(dpv, PAGES)
                    dve.wait_ge(t_full, n + 1)
                    nc.vector.tensor_copy(pdT[:, 4:8, :], T[n % 2][:, :].rearrange("p (j q) -> p j q", j=4)).then_inc(t_free["dve"], 1)
                elif kind == "DOT":
                    r, n = s[1], T_OF[s]
                    dve.wait_ge(dpv, PAGES * (r + 1))
                    if r:
                        dve.wait_ge(t_full, T_OF["DOT", 0] + 1)
                    dve.wait_ge(d_rec, r + 1)
                    nc.vector.tensor_scalar(od[:, :], O[1][:, 0:KVW], drec, 0.5, ALU.mult, ALU.mult).then_inc(od_done, 1)
                    dve.wait_ge(t_full, n + 1)
                    for hd in range(HEADS):
                        kvh, g = hd // 2, hd % 2
                        frm = (kvh % 2) * HD
                        src = T[n % 2][frm:frm + HD, (kvh // 2) * P:(kvh // 2 + 1) * P].rearrange("p (x h) -> p x h", h=HEADS)[:, :, hd]
                        ins = nc.vector.tensor_copy(att_s[g * HD:(g + 1) * HD, kvh, 16 * r:16 * r + 16], src)
                        ins.then_inc(t_free["dve"] if hd == HEADS - 1 else dve_chain, 1)
                    chain[0] += HEADS - 1
                elif kind == "VSN":
                    tt, n = s[1], T_OF[s]
                    R = ROWS[tt]
                    if tt == 0:
                        dve.wait_ge(staged[5], 128)
                        dve.wait_ge(staged[4], 128)
                    src = T[n % 2][0:R, :].rearrange("p (g c) -> p g c", g=GRP)
                    dve.wait_ge(t_full, n + 1)
                    link(nc.vector.tensor_reduce(ln_mu[0:R, 0, :], src, AX.X, ALU.add))
                    link(nc.vector.tensor_scalar(ln_mu[0:R, 1, :], ln_mu[0:R, 0, :], 1.0 / GCH, None, ALU.mult))
                    vt = vn[0:R, tt, :].rearrange("p (g c) -> p g c", g=GRP)
                    nc.vector.tensor_tensor(vt, src, ln_mu[0:R, 1, :].unsqueeze(2).broadcast_to([R, GRP, GCH]), ALU.subtract).then_inc(t_free["dve"], 1)
                    dve.wait_ge(sq_done, tt + 1)
                    nc.vector.tensor_reduce(ln_var[0:R, tt, :], ln_sq[0:R, :].rearrange("p (g c) -> p g c", g=GRP), AX.X, ALU.add).then_inc(ssq_done, 1)
                elif kind == "LN":
                    dve.wait_ge(lnstd_done, 2)
                    nc.vector.reciprocal(ln_rstd[:, 0:4, :], ln_std[:, 0:4, :]).then_inc(dve_chain, 1)
                    chain[0] += 1
                    link(nc.vector.reciprocal(ln_rstd[0:SMP, 4, :], ln_std[0:SMP, 4, :]))
                    for tt in (4, 0, 1, 2, 3):
                        R = ROWS[tt]
                        vt = vn[0:R, tt, :].rearrange("p (g c) -> p g c", g=GRP)
                        nc.vector.tensor_tensor(vt, vt, ln_rstd[0:R, tt, :].unsqueeze(2).broadcast_to([R, GRP, GCH]), ALU.mult).then_inc(lnmul_done, 1)
                elif kind == "PSC":
                    u = s[1]
                    keys = P * (UNITS[u][1] + 1)
                    dve.wait_ge(psc, u + 1)
                    if u >= 2:
                        dve.wait_ge(p_exp, 2 * u - 2)
                    nc.vector.tensor_reduce(nmax[:, u % 2, :], S[:, :].rearrange("p (g c) -> p g c", g=2)[:, :, 0:keys], AX.X, ALU.max, negate=True)\
                        .then_inc(p_max, 1)
                elif kind == "PN":
                    u = s[1]
                    keys = P * (UNITS[u][1] + 1)
                    dve.wait_ge(p_exp, 2 * u + 2)
                    link(nc.vector.reciprocal(rsum[:, u % 2, :], psums[:, u % 2, :]))
                    for g in range(2):
                        part = probs[:, u % 2, g, 0:keys]
                        nc.vector.tensor_scalar(part, part, rsum[:, u % 2, g:g + 1], 0.5, ALU.mult, ALU.mult).then_inc(p_norm, 1)
                elif kind == "PTR":
                    u, n = s[1], T_OF[s]
                    blocks = UNITS[u][1] + 1
                    for g in range(2):
                        dve.wait_ge(pT_hi_done, 2 * u + g + 1)
                        nc.vector.tensor_tensor(pT_lo[:, u % 2, 0:blocks, g, :],
                                                T[(n + g) % 2][:, 0:blocks * P].rearrange("p (j q) -> p j q", q=P),
                                                pT_hi[:, u % 2, 0:blocks, g, :].bitcast(fp32), ALU.subtract)\
                            .then_inc(t_free["dve"], 1)
                elif kind == "PPV":
                    u = s[1]
                    kvh, i = UNITS[u]
                    dve.wait_ge(o_hi, u + 1)
                    if u == 0:
                        pass
                    for g in range(2):
                        link(nc.vector.tensor_tensor(att[g * HD:(g + 1) * HD, u % 2, :], O[u % 2][0:HD, g * P:(g + 1) * P],
                                                     o_tmp[:, u % 2, g * P:(g + 1) * P], ALU.add))
                    dve.wait_ge(z_free["dve"], freed(Z_FREED_BY, 2 * TILE_OF["ga", kvh] + 1)[1])
                    part = zga[:, kvh, i * P:(i + 1) * P]
                    nc.vector.tensor_tensor(part, part, att[:, u % 2, :], ALU.mult).then_inc(att_done, 1)
                elif kind == "SP":
                    gp, n = s[1], T_OF[s]
                    dve.wait_ge(t_full, n + 1)
                    dve.wait_ge(b_in, 32)
                    if gp:
                        dve.wait_ge(t_free["dve"], freed(T_FREED_BY, T_OF["SP", gp - 1])[1])
                    link(nc.vector.tensor_tensor(sp_sum[:, :].rearrange("p (c t) -> p c t", t=P), T[n % 2][:, :].rearrange("p (c t) -> p c t", t=P),
                                                 b_bc[:, gp, :].unsqueeze(1).broadcast_to([P, 4, P]), ALU.add))
                    dve.wait_ge(ug_done, gp + 1)
                    nc.vector.scalar_tensor_tensor(zgg[:, gp, 0:SEQ], sp_sum[:, :], 0.5, zu[:, gp, 0:SEQ], ALU.mult, ALU.mult).then_inc(t_free["dve"], 1)
                elif kind == "SPS":
                    n = T_OF[s]
                    dve.wait_ge(t_full, n + 1)
                    dve.wait_ge(ug_done, 4)
                    src = T[n % 2][:, 0:4 * SMP].rearrange("p (g b t) -> p g b t", g=4, t=DEC_T)
                    tmp = sp_sum[:, 0:4 * SMP].rearrange("p (g b t) -> p g b t", g=4, t=DEC_T)
                    dve.wait_ge(t_free["dve"], freed(T_FREED_BY, T_OF["SP", 3])[1])
                    link(nc.vector.tensor_tensor(tmp, src, b_bc[:, :, 0:DEC_T].unsqueeze(2).broadcast_to([P, 4, DEC_B, DEC_T]), ALU.add))
                    nc.vector.scalar_tensor_tensor(zgg[:, :, SEQ:TOK], sp_sum[:, 0:4 * SMP].rearrange("p (g x) -> p g x", g=4), 0.5,
                                                   zu[:, :, SEQ:TOK], ALU.mult, ALU.mult).then_inc(t_free["dve"], 1)
                    dve.wait_ge(z_free["dve"], freed(Z_FREED_BY, 2 * TILE_OF["ga", 3] + 1)[1])
                    dve.wait_ge(t_free["dve"], freed(T_FREED_BY, T_OF["DOT", 1])[1])
                    nc.vector.tensor_tensor(zga[:, :, SEQ:TOK], zga[:, :, SEQ:TOK], att_s[:, :, :], ALU.mult).then_inc(gm_done, 1)
                elif kind == "MIX":
                    k = s[1]
                    dve.wait_ge(mix_hi, MIX_N[s] + 1)
                    nc.vector.tensor_tensor(act_lo[:, k, :], zga[:, k, :] if k < 4 else zgg[:, k - 4, :], act_hi[:, k, :].bitcast(fp32), ALU.subtract)\
                        .then_inc(mix_done, 1)
                elif kind == "Y":
                    c = s[1]
                    hf = OUT_CHUNKS[c][0]
                    if NT + c + 1 < NW:
                        split_lo(NT + c + 1)
                    if c % 4 == 3:
                        if c == 3:
                            dve.wait_ge(ppv, len(UNITS))
                        for tt in range(TT):
                            R = ROWS[tt]
                            dve.wait_ge(y_full, TT * c + tt + 1)
                            nc.vector.tensor_copy(y_sb[0:R, tt, hf * 512:(hf + 1) * 512], Y[hf][tt][0:R, :]).then_inc(y_out, 1)
                        if hf == 1:
                            dve.wait_ge(gpost_in, 16)
                            for tt in range(TT):
                                R = ROWS[tt]
                                dve.wait_ge(y_sq, TT + tt + 1)
                                nc.vector.tensor_tensor(y_sst[0:R, tt:tt + 1], y_ss[0:R, tt:tt + 1], y_ss[0:R, 5 + tt:6 + tt], ALU.add).then_inc(y_ssq, 1)
                                dve.wait_ge(y_std, tt + 1)
                                link(nc.vector.reciprocal(y_rs[0:R, tt:tt + 1], y_sd[0:R, tt:tt + 1]))
                                link(nc.vector.scalar_tensor_tensor(y_sb[0:R, tt, :], y_sb[0:R, tt, :], y_rs[0:R, tt:tt + 1], g_post_bc[0:R, :], ALU.mult, ALU.mult))
                                dve.wait_ge(xr_in[tt], 16)
                                nc.vector.tensor_tensor(y_sb[0:R, tt, :], y_sb[0:R, tt, :], x_res[0:R, tt, :], ALU.add).then_inc(y_done, 1)

        @block.tensor
        def _(pe):
            mm = nc.tensor.matmul

            def turn(n, col, in_, rows, out_rows):
                return nc.tensor.transpose(T[n % 2][0:out_rows, col:col + rows], in_, ident[0:rows, 0:rows])

            def ktr_in(m):
                pe.wait_ge(k_in[m % 2], 64 * (m // 2 + 1))

            pe.wait_ge(consts_made, 1)
            for s in SCHEDULE:
                kind, n = s[0], T_OF[s]
                if kind == "XT":
                    tt = s[1]
                    pe.wait_ge(xn_done, tt + 1)
                    for kk in range(2):
                        bank_free(pe, n + kk)
                        for k in range(4):
                            last = turn(n + kk, k * ROWS[tt], xn[0:ROWS[tt], tt % 2, (4 * kk + k) * P:(4 * kk + k + 1) * P], ROWS[tt], P)
                        last.then_inc(t_full, 1)
                elif kind == "Z":
                    t, half = s[1], s[2]
                    h = 2 * t + half
                    if t == 0:
                        pe.wait_ge(t_free["dve"], 6 if half == 0 else 10)
                    if half == 0:
                        pe.wait_ge(w_split, t + 1)
                    z_bank_free(pe, h)
                    cols = slice(half * HALF, (half + 1) * HALF)
                    wh, wl = w_split_tile(w_hi, t), w_split_tile(w_lo, t)
                    for k in range(KD):
                        mm(Z[h % 2][:, 0:HALF], wh[:, k, :], act_hi[:, k, cols], start=(k == 0), stop=False)
                        mm(Z[h % 2][:, 0:HALF], wh[:, k, :], act_lo[:, k, cols], start=False, stop=False)
                        last = mm(Z[h % 2][:, 0:HALF], wl[:, k, :], act_hi[:, k, cols], start=False, stop=(k == KD - 1))
                    last.then_inc(z_full, 1)
                elif kind == "WT":
                    pe.wait_ge(wsp_masked, 1)
                    for e in range(2):
                        bank_free(pe, n + e)
                        for g in range(4):
                            last = turn(n + e, g * P, wsp[:, 4 * e + g, :], P, P)
                        last.then_inc(t_full, 1)
                    bank_free(pe, n + 2)
                    pe.wait_ge(rep_done, 1)
                    by, count = freed(T_FREED_BY, n + 1)
                    pe.wait_ge(t_free[by], count)
                    mm(T[(n + 2) % 2][0:SMP, 0:GRP * DEC_T], rep4[:, :], wspT[0:DEC_T, :, 0:DEC_T], start=True, stop=True).then_inc(t_full, 1)
                elif kind == "KVN":
                    tt = s[1]
                    bank_free(pe, n)
                    if tt == 0:
                        pe.wait_ge(z_free["act"], freed(Z_FREED_BY, 2 * TILE_OF["v", 1] + 1)[1])
                        pe.wait_ge(z_hi, 12)
                    for j in range(4):
                        last = turn(n, j * P, kv32[:, j, tokens(tt)], P, ROWS[tt])
                    last.then_inc(t_full, 1)
                elif kind == "KTR":
                    _, r, kk, b = s
                    ktr_in(KTR_N[s])
                    for c in range(2):
                        bank_free(pe, n + c)
                        for j in range(4):
                            last = turn(n + c, j * P, k_ring[:, KTR_N[s] % 2, j, c * P:(c + 1) * P], P, P)
                        last.then_inc(t_full, 1)
                elif kind == "DSC":
                    r, kk = s[1], s[2]
                    if r == 0 and kk == 0:
                        pe.wait_ge(qbd_done, 1)
                    for e in range(2):
                        by, count = freed(T_FREED_BY, T_OF["KTR", r, kk, 3] + e)
                        pe.wait_ge(t_free[by], count)
                    if r:
                        pe.wait_ge(d_exp, r)
                    for c in range(2):
                        for b in range(4):
                            last = mm(S[32 * b:32 * b + 32, kk * 512:(kk + 1) * 512], qbd[:, c, r, 32 * b:32 * b + 32], kT[:, c, b, :],
                                      start=(c == 0), stop=(c == 1))
                    last.then_inc(dsc, 1)
                elif kind == "DOWN":
                    r = s[1]
                    pe.wait_ge(z_hi, 12)
                    if r:
                        pe.wait_ge(d_bias, r)
                    for c in range(2):
                        last = mm(O[0][:, 0:SMP], qbd[:, c, r, :], kv32[:, c, SEQ:TOK], start=(c == 0), stop=(c == 1))
                    last.then_inc(down, 1)
                elif kind == "DPT":
                    r = s[1]
                    pe.wait_ge(d_exp, r + 1)
                    for e in range(2):
                        bank_free(pe, n + e)
                        for j in range(4):
                            last = turn(n + e, j * P, pd[:, (4 * e + j) * P:(4 * e + j + 1) * P], P, P)
                        last.then_inc(t_full, 1)
                    bank_free(pe, n + 2)
                    nc.tensor.transpose(T[(n + 2) % 2][0:SMP, 0:P], p_own[:, :], ident[:, :]).then_inc(t_full, 1)
                elif kind == "DPV":
                    r, part = s[1], s[2]
                    if part == 0:
                        for e in range(3):
                            by, count = freed(T_FREED_BY, T_OF["DPT", r] + e)
                            pe.wait_ge(t_free[by], count)
                        if r:
                            pe.wait_ge(od_done, r)
                        mm(O[1][:, 0:KVW], p_ownT[:, :], kv_s[:, KVW:2 * KVW], start=True, stop=False, skip_group_check=True)
                    for pg in range(4 * part, 4 * part + 4):
                        m = r * PAGES + pg
                        pe.wait_ge(v_in[m % 4], 64 * (m // 4 + 1))
                        for b in range(4):
                            last = mm(O[1][32 * b:32 * b + 32, 0:KVW], pdT[:, pg, 32 * b:32 * b + 32], v_ring[:, m % 4, b, :],
                                      start=False, stop=(pg == PAGES - 1), skip_group_check=True)
                        last.then_inc(dpv, 1)
                elif kind == "DOT":
                    r = s[1]
                    bank_free(pe, n)
                    pe.wait_ge(od_done, r + 1)
                    for c in range(2):
                        last = turn(n, c * P, od[:, c * P:(c + 1) * P], P, P)
                    last.then_inc(t_full, 1)
                elif kind == "VSN":
                    tt = s[1]
                    bank_free(pe, n)
                    if tt == 0:
                        pe.wait_ge(z_free["act"], freed(Z_FREED_BY, 2 * TILE_OF["vs", 3] + 1)[1])
                    for j in range(4):
                        last = turn(n, j * P, zvs[:, j, tokens(tt)], P, ROWS[tt])
                    last.then_inc(t_full, 1)
                elif kind == "PSC":
                    u = s[1]
                    kvh, i = UNITS[u]
                    if i == 0:
                        pe.wait_ge(staged[kvh], 64)
                        pe.wait_ge(staged[4 + kvh // 2], 128)
                    if u == 0:
                        pe.wait_ge(d_exp, 2)
                    else:
                        pe.wait_ge(p_exp, 2 * u)
                    keys = max(2 * P, P * (i + 1))
                    for g in range(2):
                        out = S[:, g * 512:g * 512 + keys]
                        q = q_st[:, 2 * kvh + g, i * P:(i + 1) * P]
                        mm(out, q, k_hi[:, kvh, 0:keys], start=True, stop=False)
                        mm(S[:, g * 512 + i * P:g * 512 + (i + 1) * P], ident_h[:, :], causal[:, :], start=False, stop=False, skip_group_check=True)
                        last = mm(out, q, k_lo[:, kvh, 0:keys], start=False, stop=True)
                    last.then_inc(psc, 1)
                elif kind == "PTR":
                    u = s[1]
                    for g in range(2):
                        pe.wait_ge(p_norm, 2 * u + g + 1)
                        bank_free(pe, n + g)
                        for j in range(UNITS[u][1] + 1):
                            last = turn(n + g, j * P, probs[:, u % 2, g, j * P:(j + 1) * P], P, P)
                        last.then_inc(t_full, 1)
                elif kind == "PPV":
                    u = s[1]
                    kvh, i = UNITS[u]
                    by, count = freed(T_FREED_BY, T_OF["PTR", u] + 1)
                    pe.wait_ge(t_free[by], count)
                    if u == 0:
                        pe.wait_ge(vst_done, 4)
                        pe.wait_ge(d_bias, 2)
                    elif u == 1:
                        pe.wait_ge(od_done, 2)
                    else:
                        pe.wait_ge(att_done, u - 1)
                    for j in range(i + 1):
                        for e, part in enumerate((pT_hi, pT_lo)):
                            last = mm(O[u % 2][:, 0:256], v_st[:, j, kvh, :], part[:, u % 2, j, :, :].rearrange("p g q -> p (g q)"),
                                      start=(j == 0 and e == 0), stop=(j == i and e == 1))
                    last.then_inc(ppv, 1)
                elif kind == "SP":
                    gp = s[1]
                    bank_free(pe, n)
                    pe.wait_ge(vn_done, TT)
                    for c in range(4):
                        for e in range(2):
                            g = 2 * gp + e
                            last = mm(T[n % 2][e * HD:(e + 1) * HD, c * P:(c + 1) * P], vn[:, c, g * GCH:(g + 1) * GCH], wspT[:, g, :], start=True, stop=True)
                    last.then_inc(t_full, 1)
                elif kind == "SPS":
                    bank_free(pe, n)
                    pe.wait_ge(t_free["dve"], freed(T_FREED_BY, T_OF["WT",] + 2)[1])
                    for g in range(GRP):
                        e, gp = g % 2, g // 2
                        last = mm(T[n % 2][e * HD:(e + 1) * HD, gp * SMP:(gp + 1) * SMP], vn[0:SMP, 4, g * GCH:(g + 1) * GCH], w_bd[:, g, :], start=True, stop=True)
                    last.then_inc(t_full, 1)
                elif kind == "Y":
                    c = s[1]
                    hf, kp = OUT_CHUNKS[c]
                    pe.wait_ge(w_split, NT + c + 1)
                    if hf == 0:
                        pe.wait_ge(mix_done, max(MIX_N["MIX", 2 * kp], MIX_N["MIX", 2 * kp + 1]) + 1)
                    if c == 0:
                        pe.wait_ge(z_free["dve"], freed(Z_FREED_BY, 2 * NT - 1)[1])
                        pe.wait_ge(p_exp, 2 * len(UNITS))
                        for use in (len(T_FREED_BY) - 2, len(T_FREED_BY) - 1):
                            by, count = freed(T_FREED_BY, use)
                            pe.wait_ge(t_free[by], count)
                    if c == 4:
                        pe.wait_ge(att_done, len(UNITS))
                        pe.wait_ge(y_out, 2)
                    first, end = c % 4 == 0, c % 4 == 3
                    for tt in range(TT):
                        R = ROWS[tt]
                        for e in range(2):
                            k = 2 * kp + e
                            wh, wl = w_hi[:, (NT + c) % 2, e * 512:(e + 1) * 512], w_lo[:, (NT + c) % 2, e * 512:(e + 1) * 512]
                            mm(Y[hf][tt][0:R, :], act_hi[:, k, tokens(tt)], wh, start=(first and e == 0), stop=False)
                            mm(Y[hf][tt][0:R, :], act_lo[:, k, tokens(tt)], wh, start=False, stop=False)
                            last = mm(Y[hf][tt][0:R, :], act_hi[:, k, tokens(tt)], wl, start=False, stop=(end and e == 1))
                        last.then_inc(y_full, 1)
    return nc


_INS = ["x_prompt", "x_sample", "cache_k", "cache_v", "page_table", "g_pre", "w_in", "g_sgu",
        "w_spatial", "b_spatial", "w_out", "g_post"]
_OUTS = [(1, SEQ, D), (DEC_B, DEC_T, D), (1, 1, SEQ, KVH, HD), (1, 1, SEQ, KVH, HD),
         (1, DEC_B, DEC_T, KVH, HD), (1, DEC_B, DEC_T, KVH, HD), (1, DEC_B, DEC_T, GRP * GCH)]


def kernel(**inputs):
    import numpy as np
    import concourse.bacc as bacc
    from concourse.bass_utils import run_bass_kernel_spmd

    nc = bacc.Bacc("TRN2", target_bir_lowering=False, num_devices=1)
    arrays, args = {}, []
    for name in _INS:
        a = np.ascontiguousarray(inputs[name])
        arrays[f"in_{name}"] = a
        args.append(nc.dram_tensor(f"in_{name}", a.shape, mybir.dt.from_np(a.dtype), kind="ExternalInput").ap())
    for n, shape in enumerate(_OUTS):
        args.append(nc.dram_tensor(f"out_{n}", shape, fp32, kind="ExternalOutput").ap())
    build(nc, *args)
    r = run_bass_kernel_spmd(nc, [arrays], core_ids=[0])
    return tuple(r.results[0][f"out_{n}"] for n in range(len(_OUTS)))
```

```python
from contextlib import ExitStack

import concourse.bass as bass
from concourse import mybir

fp32 = mybir.dt.float32
f32r = mybir.dt.float32r
bf16 = mybir.dt.bfloat16
i32 = mybir.dt.int32
ALU = mybir.AluOpType
ACT = mybir.ActivationFunctionType
AX = mybir.AxisListType

P = 128
D = 1024
KD = D // P
SEQ, DEC_B, DEC_T = 512, 8, 4
SMP = DEC_B * DEC_T
TOK = SEQ + SMP
HALVES = [slice(0, SEQ // 2), slice(SEQ // 2, TOK)]
WIDE = TOK - SEQ // 2
MIX_COLS = [slice(0, SEQ // 2), slice(SEQ // 2, SEQ)]
HEADS, KVH, HD = 8, 4, 64
KVW = KVH * HD
PAGE, PAGES = 128, 8
BLOCK = 256
NBLK = PAGE * PAGES // BLOCK
GRP, GCH = 8, 64
NEG = -1.0e30
RMS_EPS, LN_EPS = 1e-6, 1e-5
QSCALE = HD ** -0.5

Q_T, K_T, V_T, GA_T, U_T, VS_T, GG_T = 0, 4, 6, 8, 12, 16, 20
ORDER = ([("q", j, Q_T + j) for j in range(4)] + [("k", j, K_T + j) for j in range(2)]
         + [("v", j, V_T + j) for j in range(2)] + [("vs", j, VS_T + j) for j in range(4)]
         + [("u", j, U_T + j) for j in range(4)] + [("ga", j, GA_T + j) for j in range(4)]
         + [("gg", j, GG_T + j) for j in range(4)])
NT = len(ORDER)
TILE_OF = {(kind, j): n for n, (kind, j, _) in enumerate(ORDER)}
OUT_CHUNKS = [(hf, kp) for hf in range(2) for kp in range(4)]
NW = NT + len(OUT_CHUNKS)
TT = 5
ROWS = [P] * 4 + [SMP]
Y_ORDER = [4, 0, 1, 2, 3]
UNITS = [(kvh, i) for kvh in range(KVH) for i in range(4)]


def schedule():
    s = [("XT", tt) for tt in range(TT)] + [("Z", 0, 0), ("ZE", 0, 0), ("Z", 0, 1), ("ZE", 0, 1)]
    side = {}

    def after(n, *steps):
        side.setdefault(n, []).extend(steps)

    for b in range(4):
        after(1 + b, ("KTR", 0, 0, b))
    after(5, ("WT",))
    after(6, ("WB",))
    after(8, ("DSC", 0, 0))
    for b in range(4):
        after(8 + b, ("KTR", 0, 1, b))
    after(12, ("DSC", 0, 1), ("DOWN", 0), ("KTR", 1, 0, 0), ("DSM", 0))
    for b in range(1, 4):
        after(12 + b, ("KTR", 1, 0, b))
    after(14, ("DEX", 0))
    after(16, ("DPT", 0))
    after(16, ("KVN", 0), ("KVN", 4), ("DSC", 1, 0), ("DOWN", 1))
    for n in range(3):
        after(17 + n, ("KVN", 1 + n))
    for b in range(4):
        after(16 + b, ("KTR", 1, 1, b))
    for pg in range(8):
        after(16 + pg * 3 // 4, ("DPV", 0, pg))
    after(20, ("DSC", 1, 1), ("DSM", 1))
    after(21, ("DEX", 1))
    after(22, ("DOD", 0))
    after(23, ("DOT", 0))
    after(23, ("DPT", 1))
    for n in range(TT):
        after(24 + n, ("VSN", n))
    after(29, ("LN",))
    for n, tt in enumerate((4, 0, 1, 2, 3)):
        after(31 + 2 * n, ("LNM", tt))
    for pg in range(8):
        after(24 + pg * 3 // 4, ("DPV", 1, pg))
    after(30, ("DOD", 1), ("DOT", 1))
    after(40, ("AS",))
    first = 30
    for h in range(first, 2 * NT):
        u = h - first
        if h in [2 * TILE_OF["gg", gp] + 3 for gp in range(3)]:
            after(h, ("SP", (h - 3) // 2 - TILE_OF["gg", 0]))
        if u < len(UNITS):
            after(h, ("PSC", u), ("PN", u))
        if u == len(UNITS):
            after(h, ("PTR", u - 1))
        if 2 <= u < len(UNITS) + 2:
            after(h, ("PPV", u - 2))
        if 1 <= u < len(UNITS):
            after(h, ("PTR", u - 1))
        after(h, ("ZE", h // 2, h % 2))
        if 2 <= u < len(UNITS) + 2:
            after(h, ("ATT", u - 2))
    after(2 * NT - 2, ("MIX", 0, 0), ("MIX", 1, 0))
    s += side.get(1, [])
    for h in range(2, 2 * NT):
        s.append(("Z", h // 2, h % 2))
        if h < first:
            s.append(("ZE", h // 2, h % 2))
        s += side.get(h, [])
    s += [("MIX", 0, 1), ("MIX", 1, 1), ("MIX", 2, 0), ("MIX", 2, 1), ("MIX", 3, 0), ("MIX", 3, 1)]
    s += [("SP", 3), ("SPS",), ("YS", 0), ("Y", 0), ("MIX", 4, 0), ("MIX", 4, 1), ("MIX", 5, 0), ("MIX", 5, 1),
          ("YS", 1), ("Y", 1), ("MIX", 6, 0), ("MIX", 6, 1), ("MIX", 7, 0), ("MIX", 7, 1),
          ("YF", 0), ("Y", 2), ("YS", 2), ("Y", 3), ("YS", 3), ("YH",), ("YF", 1)]
    s += [("Y2", tt) for tt in Y_ORDER]
    return s


SCHEDULE = schedule()

T_OF, T_FREED_BY = {}, []
for _s in SCHEDULE:
    _by = {"KTR": ["act", "dve"], "WT": ["act", "act"], "WB": ["dve"], "KVN": ["act"],
           "DPT": ["act", "dve", "act"], "DOT": ["dve"], "VSN": ["dve"], "PTR": ["dve", "dve"],
           "SP": ["dve"], "SPS": ["dve"]}.get(_s[0], [])
    T_OF[_s] = len(T_FREED_BY)
    T_FREED_BY.extend(_by)


def freed(uses, n):
    return uses[n], sum(x == uses[n] for x in uses[:n + 1])


Z_FREED_BY = [{"q": "dve", "k": "dve", "v": "act", "vs": "act", "u": "act", "ga": "dve", "gg": "dve"}[kind]
              for kind, _, _ in ORDER for _ in range(2)]


HALF_BEFORE = {}
_h = -1
for _s in SCHEDULE:
    _h = 2 * _s[1] + _s[2] if _s[0] == "Z" else _h
    HALF_BEFORE[_s] = _h


OUT_SPLITS = {("Y", 0): [1], ("Y", 1): [2, 4], ("Y", 2): [3, 5], ("Y", 3): [6], ("YS", 3): [7]}
SPLIT_ORDER = list(range(NT + 1)) + [NT + c for s_ in OUT_SPLITS.values() for c in s_]
GATE_HALVES = [2 * n + half for n, o in enumerate(ORDER) if o[0] in ("ga", "gg") for half in range(2)]


def lo_by(n):
    return "pool" if n < 2 or 13 <= n <= NT else "dve"


def split_count(n):
    return SPLIT_ORDER.index(n) + 1


def lo_count(n):
    return sum(lo_by(m) == lo_by(n) for m in SPLIT_ORDER[:split_count(n)])


def w_load_count(n):
    return sum(16 if 2 * m < NT else 32 for m in range(n // 2 % 2, n // 2 + 1, 2) if m)


def position(kind):
    return {s: n for n, s in enumerate(s for s in SCHEDULE if s[0] == kind)}


KTR_N = position("KTR")
MIX_N = position("MIX")
LNM_N = position("LNM")


def tokens(tt):
    return slice(tt * P, tt * P + ROWS[tt])


def build(nc, x_prompt, x_sample, cache_k, cache_v, page_table, g_pre, w_in, g_sgu, w_spatial,
          b_spatial, w_out, g_post, y_prompt, y_sample, k_prompt, v_prompt, k_sample, v_sample,
          sgu_sample):
    n_phys = cache_k.shape[1]
    x_src = [x_prompt[0, tokens(tt), :] for tt in range(4)] + [x_sample.rearrange("b t d -> (b t) d")]
    y_dst = [y_prompt[0, tokens(tt), :] for tt in range(4)] + [y_sample.rearrange("b t d -> (b t) d")]
    w_in_v = w_in[0].rearrange("(k p) c -> p k c", p=P)
    w_out_v = w_out[0].rearrange("(k p) c -> p k c", p=P)

    def kv_rows(prompt, sample, tt):
        if tt < 4:
            return prompt[0, 0, tokens(tt)].rearrange("s h d -> s (h d)")
        return sample[0].rearrange("b t h d -> (b t) (h d)")

    with ExitStack() as ctx:
        def sem(name):
            return ctx.enter_context(nc.semaphore(name))

        top = [-(-nc.sbuf_base // 32) * 32]

        def region(size):
            at = top[0]
            top[0] += size
            return at

        def place(name, shape, dt, at):
            return nc.alloc_sbuf_tensor_at(name, shape, dt, offset=at)

        R_H = region(2 * KD * TOK * 4)
        act_hi = place("act_hi", [P, KD, TOK], f32r, R_H)
        act_lo = place("act_lo", [P, KD, TOK], f32r, R_H + KD * TOK * 4)
        ZB = 4 * TOK * 4
        R_Z = region(3 * ZB)
        zu = place("zu", [P, 4, TOK], fp32, R_Z)
        zvs = place("zvs", [P, 4, TOK], fp32, R_Z + ZB)
        zga = place("zga", [P, 4, TOK], fp32, R_Z + ZB)
        kv32 = place("kv32", [P, 4, TOK], fp32, R_Z + 2 * ZB)
        zgg = place("zgg", [P, 4, TOK], fp32, R_Z + 2 * ZB)
        wsp = place("wsp", [P, GRP, P], fp32, R_Z + ZB)
        R_W = region(16384 + 16384)
        w_raw = place("w_raw", [P, 2, 2 * D], fp32, R_W)
        w_hi = place("w_hi", [P, 2, D], f32r, R_W + 16384)
        w_lo = place("w_lo", [P, 2, D], f32r, R_W + 24576)
        R_Q = region(32768)
        x_sb = place("x_sb", [P, TT, D], fp32, R_Q)
        xn = place("xn", [P, 3, D], fp32, R_Q + 20480)
        q_st = place("q_st", [P, HEADS, SEQ], f32r, R_Q)
        k_hi = place("k_hi", [P, KVH, SEQ], f32r, R_Q + 16384)
        k_lo = place("k_lo", [P, KVH, SEQ], f32r, R_Q + 24576)
        x_res = place("x_res", [P, TT, D], fp32, R_Q)
        y_part = place("y_part", [SMP, 3, 512], fp32, R_Q + 20480)
        y_sum = place("y_sum", [SMP, 2, 512], fp32, R_Q + 26624)
        R_V = region(4096 + 8192 + 10240)
        kvn = place("kvn", [P, 2, 512], fp32, R_V)
        ln_sq = place("ln_sq", [P, 512], fp32, R_V)
        g_sgu_bc = place("g_sgu_bc", [P, 512], fp32, R_V + 2048)
        w2_hi = place("w2_hi", [P, 2, D], f32r, R_V + 4096)
        w2_lo = place("w2_lo", [P, 2, D], f32r, R_V + 12288)
        v_st = place("v_st", [P, 4, KVH, 2 * HD], f32r, R_V + 4096)
        vn = place("vn", [P, TT, 512], fp32, R_V + 12288)
        R_D = region(8192 + 16384 + 16384 + 4096 + 4096)
        k_ring = place("k_ring", [P, 2, 4, KVW], fp32, R_D)
        x_sq = place("x_sq", [P, D], fp32, R_D + 8192)
        k_ring2 = place("k_ring2", [P, 2, 4, KVW], fp32, R_V + 12288)
        kT = place("kT", [P, 2, 4, 512], fp32, R_D + 8192)
        v_ring = place("v_ring", [P, 4, 4, KVW], fp32, R_D + 24576)
        qk_hi = place("qk_hi", [P, 2, SEQ], f32r, R_D + 40960)
        qk_lo = place("qk_lo", [P, 2, SEQ], f32r, R_D + 45056)
        g_pre_bc = place("g_pre_bc", [P, D], fp32, R_D + 24576)
        pd = place("pd", [P, PAGE * PAGES], fp32, R_D + 40960)
        pdT = place("pdT", [P, PAGES, P], fp32, R_D + 45056)
        probs = place("probs", [P, 2, 2, SEQ], fp32, R_D)
        pT_hi = place("pT_hi", [P, 2, 4, 2, P], f32r, R_D + 8192)
        pT_lo = place("pT_lo", [P, 2, 4, 2, P], f32r, R_D + 16384)
        y_sb = place("y_sb", [P, TT, D], fp32, R_D)
        g_post_bc = place("g_post_bc", [P, D], fp32, R_D + 24576)
        b_bc = place("b_bc", [P, 4, P], fp32, R_D + 28672)
        th = place("th", [P, 2, WIDE], fp32, R_D + 40960)
        att = place("att", [P, 2, P], fp32, R_D + 43264)
        o_tmp = place("o_tmp", [HD, 2, 256], fp32, R_D + 45056)
        sp_sum = place("sp_sum", [P, 512], fp32, R_D + 47104)

        def small(name, shape, dt=fp32):
            size = 1
            for d in shape[1:]:
                size *= d
            return place(name, shape, dt, region(-(-size * (2 if dt == bf16 else 4) // 32) * 32))

        ident = small("ident", [P, P])
        ident_h = small("ident_h", [P, P], bf16)
        causal = small("causal", [P, P], bf16)
        wspT = small("wspT", [P, GRP, P])
        own_mask = small("own_mask", [P, 2, SMP])
        bd_mask = small("bd_mask", [SMP, DEC_B, DEC_T])
        rep4 = small("rep4", [DEC_T, SMP])
        w_bd = small("w_bd", [SMP, GRP, SMP])
        pages_i = small("pages_i", [1, DEC_B * PAGES], i32)
        qbd = small("qbd", [P, 2, 2, P])
        q_s = small("q_s", [P, 4, SMP])
        att_s = q_s
        kv_s = small("kv_s", [SMP, 512])
        od = small("od", [P, KVW])
        p_own = small("p_own", [P, SMP])
        p_ownT = small("p_ownT", [SMP, P])
        own_s = small("own_s", [P, SMP])
        rank4 = small("rank4", [P, 4])
        stat = small("stat", [P, 64])
        ln_mu = small("ln_mu", [P, 2, GRP])
        ln_var = small("ln_var", [P, TT, GRP])
        ln_std = small("ln_std", [P, TT, GRP])
        ln_rstd = small("ln_rstd", [P, TT, GRP])
        nmax = small("nmax", [P, 2, 2])
        psums = small("psums", [P, 2, 2])
        rsum = small("rsum", [P, 2, 2])
        assert top[0] <= nc.sbuf_usable_end, (top[0], nc.sbuf_usable_end)
        x_ss, x_sd, x_rs = stat[:, 0:5], stat[:, 5:10], stat[:, 10:15]
        y_ss, y_sd, y_rs = stat[:, 15:25], stat[:, 25:30], stat[:, 30:35]
        gsum, bmax, wdrop, drop, bmsk, bbias = (stat[:, 35 + 4 * n:39 + 4 * n] for n in range(6))
        gmin, wmax, omax, tmax = (stat[:, 59 + n:60 + n] for n in range(4))
        dstat = small("dstat", [P, 16])
        table_in = stat[:, 63:64]
        nm_d, dsum, dtot, drec0, y_b = dstat[:, 0:1], dstat[:, 1:6], dstat[:, 6:7], dstat[:, 7:8], dstat[:, 8:13]
        drec = [drec0, dstat[:, 13:14]]
        assert top[0] <= nc.sbuf_usable_end, (top[0], nc.sbuf_usable_end)

        def psum(name, cols):
            return ctx.enter_context(nc.psum_tensor(name, [P, cols], fp32))

        Z = [psum("Z0", 512), psum("Z1", 512)]
        T = [psum("T0", 512), psum("T1", 512)]
        S = psum("S", 1024)
        O = [psum("O0", 512), psum("O1", 512)]
        X_BANK = [[S[:, 0:512], S[:, 512:1024]], [O[0][:, :], O[1][:, :]], [T[0][:, :], T[1][:, :]],
                  [S[:, 0:512], S[:, 512:1024]], [Z[1][:, 0:256], Z[1][:, 256:512]]]
        Y = [[Z[0][:, :], S[:, 0:512], S[:, 512:1024], Z[1][:, :], O[0][:, :]],
             [T[1][:, :], O[1][:, :], Z[0][:, :], S[:, 0:512], T[0][:, :]]]

        x_in = [sem(f"x_in{t}") for t in range(TT)]
        xr_in = [sem(f"xr_in{t}") for t in range(TT)]
        gpre_in, wsp_in, b_in, gsgu_in, pages_in, gpost_in = (
            sem(n) for n in ("gpre_in", "wsp_in", "b_in", "gsgu_in", "pages_in", "gpost_in"))
        w_in_s = [sem("w_in0"), sem("w_in1")]
        w_first = [sem("w_first0"), sem("w_first1")]
        k_in = [sem(f"k_in{n}") for n in range(4)]
        v_in = [sem(f"v_in{n}") for n in range(4)]
        staged = [sem(f"staged{n}") for n in range(6)]
        stored_kv = [sem("stored_kv0"), sem("stored_kv1")]
        stored_kvs = sem("stored_kvs")
        stored, stored_sgu = sem("stored"), sem("stored_sgu")
        consts_made = sem("consts_made")
        pool_step = sem("pool_step")
        wsp_masked = sem("wsp_masked")
        vn_done = sem("vn_done")
        ug_done = sem("ug_done")
        x_std = sem("x_std")
        xn_done = sem("xn_done")
        xt_full = sem("xt_full")
        x_hi = sem("x_hi")
        x_split = sem("x_split")
        w_hi_done = sem("w_hi_done")
        w_split = {"dve": sem("w_split_dve"), "pool": sem("w_split_pool")}
        z_full = sem("z_full")
        z_free = {"act": sem("z_free_act"), "dve": sem("z_free_dve")}
        z_hi = sem("z_hi")
        t_full = sem("t_full")
        t_free = {"act": sem("t_free_act"), "dve": sem("t_free_dve")}
        vst_hi, vst_done = sem("vst_hi"), sem("vst_done")
        rep_done = sem("rep_done")
        qbd_done = sem("qbd_done")
        dsc, down = sem("dsc"), sem("down")
        d_bias = sem("d_bias")
        d_exp = sem("d_exp")
        d_rec = sem("d_rec")
        dpv = sem("dpv")
        od_done = sem("od_done")
        as_done = sem("as_done")
        psc = sem("psc")
        p_max = sem("p_max")
        p_exp = sem("p_exp")
        p_norm = sem("p_norm")
        pT_hi_done = sem("pT_hi_done")
        ppv = sem("ppv")
        o_hi = sem("o_hi")
        att_done = sem("att_done")
        sq_done, ssq_done, lnstd_done, lnmul_done = (sem(n) for n in ("sq_done", "ssq_done", "lnstd_done", "lnmul_done"))
        sp_done = sem("sp_done")
        mix_hi, mix_done = sem("mix_hi"), sem("mix_done")
        y_full = sem("y_full")
        ys = sem("ys")
        y_parts, y_fold = sem("y_parts"), sem("y_fold")
        y_sq = sem("y_sq")
        y_out = sem("y_out")
        y_bias = sem("y_bias")
        y_std = sem("y_std")
        y_done = sem("y_done")
        dve_chain = sem("dve_chain")
        act_chain = sem("act_chain")

        def k_slot(m):
            return k_ring[:, m % 2, :, :] if m % 4 < 2 else k_ring2[:, m % 2, :, :]

        def bank_free(eng, n):
            if n >= 2:
                by, count = freed(T_FREED_BY, n - 2)
                eng.wait_ge(t_free[by], count)

        def z_bank_free(eng, h):
            if h >= 2:
                by, count = freed(Z_FREED_BY, h - 2)
                eng.wait_ge(z_free[by], count)

        def y_src(hf, tt):
            return Y[hf][tt] if tt < 4 else y_sum[:, hf, :]

        def mixed(k, cs):
            return zga[:, k, cs] if k < KVH else zgg[:, k - KVH, cs]

        def mix_ready(eng, k, half):
            eng.wait_ge(z_full, 2 * NT - 1 + half)
            if k < KVH:
                eng.wait_ge(att_done, 4 * k + 2 + 2 * half)
            else:
                eng.wait_ge(sp_done, k - KVH + 1)

        def w_slot_free(eng, n):
            c = n - NT
            if c in (4, 5):
                eng.wait_ge(ppv, len(UNITS))
                eng.wait_ge(t_full, T_OF["SPS",] + 1)
                eng.wait_ge(stored_sgu, 16)
            elif c in (6, 7):
                eng.wait_ge(y_full, 4 * (c - 3))
            elif c in (2, 3):
                eng.wait_ge(y_full, 4 * (c - 1))
            elif n >= 2:
                eng.wait_ge(z_full, 2 * (n - 1))

        def w_tile(n):
            if n < NT:
                return w_raw[:, n // 2 % 2, :].rearrange("p (k c) -> p k c", k=KD)[:, :, (n % 2) * P:(n % 2 + 1) * P]
            return w_raw[:, n // 2 % 2, (n % 2) * D:(n % 2 + 1) * D]

        def w_split_tile(hi, n):
            if n < NT:
                return (w_hi if hi else w_lo)[:, n % 2, :].rearrange("p (k c) -> p k c", k=KD)
            if n - NT in (4, 5):
                return (w2_hi if hi else w2_lo)[:, n % 2, :]
            return (w_hi if hi else w_lo)[:, n % 2, :]

        block = ctx.enter_context(nc.Block())

        @block.sync
        def _(sp):
            sp.dma_start(x_sb[:, 0, :], x_src[0]).then_inc(x_in[0], 16)
            sp.dma_start(g_pre_bc[:, :], g_pre[0:1, :].broadcast_to([P, D])).then_inc(gpre_in, 16)
            sp.dma_start(x_sb[:, 1, :], x_src[1]).then_inc(x_in[1], 16)

            def load_w(m):
                if m >= 2:
                    for n in (2 * m - 4, 2 * m - 3):
                        sp.wait_ge(w_split[lo_by(n)], lo_count(n))
                    if 2 * (m - 2) >= NT:
                        sp.wait_ge(ys, m - 1 - NT // 2)
                if 2 * m < NT:
                    col = ORDER[2 * m][2] * P
                    dst, src = w_raw[:, m % 2, :].rearrange("p (k c) -> p k c", k=KD), w_in_v[:, :, col:col + 2 * P]
                    sp.dma_start(dst, src).then_inc(w_in_s[m % 2], 16)
                else:
                    for e in range(2):
                        hf, kp = OUT_CHUNKS[2 * m - NT + e]
                        dst = w_raw[:, m % 2, e * D:(e + 1) * D].rearrange("p (k c) -> p k c", k=2)
                        sp.dma_start(dst, w_out_v[:, 2 * kp:2 * kp + 2, hf * 512:(hf + 1) * 512]).then_inc(w_in_s[m % 2], 16)

            def pages(b, part):
                at = b * PAGES + 4 * part
                return nc.values_load_multi_w_load_instructions(pages_i[0:1, at:at + 4], engines=(mybir.EngineType.SP,),
                                                                min_val=0, max_val=n_phys - 1)[1]

            def load_k(m):
                r, kk, b = m // 8, m // 4 % 2, m % 4
                if m >= 4:
                    sp.wait_ge(t_full, T_OF["KTR", (m - 4) // 8, (m - 4) // 4 % 2, (m - 4) % 4] + 2)
                for j, at in enumerate(pages(4 * r + b, kk)):
                    sp.dma_start(k_slot(m)[:, j, :], cache_k[0, bass.ds(at, 1)].rearrange("a s h d -> (a s) (h d)"))\
                        .then_inc(k_in[m % 4], 16)

            def load_v(m):
                r, pg = m // PAGES, m % PAGES
                if m >= 4:
                    sp.wait_ge(dpv, m - 3)
                if pg % 4 == 0:
                    v_pages[:] = [pages(4 * r + b, pg // 4) for b in range(4)]
                for b in range(4):
                    at = v_pages[b][pg % 4]
                    sp.dma_start(v_ring[:, m % 4, b, :], cache_v[0, bass.ds(at, 1)].rearrange("a s h d -> (a s) (h d)"))\
                        .then_inc(v_in[m % 4], 16)

            def load_first(e):
                dst = w_raw[:, 0, :].rearrange("p (k c) -> p k c", k=KD)[:, :, e * P:(e + 1) * P]
                sp.dma_start(dst, w_in_v[:, :, e * P:(e + 1) * P]).then_inc(w_first[e], 16)

            load_first(0)
            for tt in (2, 3, 4):
                sp.dma_start(x_sb[0:ROWS[tt], tt, :], x_src[tt]).then_inc(x_in[tt], 16)
            load_first(1)
            sp.dma_start(pages_i[:, :], page_table.rearrange("(o b) p -> o (b p)", o=1)).then_inc(pages_in, 16)
            load_w(1)
            sp.wait_ge(pages_in, 16)
            for m in range(4):
                load_k(m)
            v_pages = []
            queue = []
            for m in range(2, NW // 2):
                queue.append((2 * (2 * m - 4) + 0.1 if 2 * m < NT + 6 else 2 * NT + 1, load_w, m))
            for m in range(4, 16):
                step = ("KTR", (m - 4) // 8, (m - 4) // 4 % 2, (m - 4) % 4)
                queue.append((HALF_BEFORE[step] + 0.5, load_k, m))
            for m in range(16):
                if m < 4:
                    queue.append((6.8, load_v, m))
                else:
                    step = ("DPV", (m - 4) // 8, (m - 4) % 8)
                    queue.append((HALF_BEFORE[step] + 0.6, load_v, m))
            queue.sort(key=lambda q: q[0])
            rest_at = HALF_BEFORE["PSC", 15] + 0.7
            done_x = False
            for at, load, m in queue:
                if at > rest_at and not done_x:
                    done_x = True
                    sp.wait_ge(psc, 2 * len(UNITS))
                    for tt in range(TT):
                        sp.dma_start(x_res[0:ROWS[tt], tt, :], x_src[tt]).then_inc(xr_in[tt], 16)
                load(m)
            for n, tt in enumerate(Y_ORDER):
                for hf in range(2):
                    sp.wait_ge(y_done, 2 * n + hf + 1)
                    cs = slice(hf * 512, (hf + 1) * 512)
                    sp.dma_start(y_dst[tt][:, cs], y_sb[0:ROWS[tt], tt, cs]).then_inc(stored, 16)
            sp.wait_ge(stored, 16 * 2 * TT)
            sp.wait_ge(stored_sgu, 16)
            for n in range(2):
                sp.wait_ge(stored_kv[n], 2 * 32)
            sp.wait_ge(stored_kvs, 32)

        @block.gpsimd
        def _(pool):
            count = [0]

            def link(ins):
                count[0] += 1
                ins.then_inc(pool_step, 1)
                pool.wait_ge(pool_step, count[0])

            nc.gpsimd.memset(ident[:, :], 0.0).then_inc(pool_step, 1)
            nc.gpsimd.memset(ident_h[:, :], 0.0).then_inc(pool_step, 1)
            nc.gpsimd.memset(causal[:, :], 0.0).then_inc(pool_step, 1)
            nc.gpsimd.memset(own_mask[:, :, :], 0.0).then_inc(pool_step, 1)
            nc.gpsimd.memset(bd_mask[:, :, :], 1.0).then_inc(pool_step, 1)
            count[0] = 5
            pool.wait_ge(pool_step, 5)

            def select(t, pattern, op, fill, base, mult):
                link(nc.gpsimd.affine_select(out=t, in_=t, pattern=pattern, compare_op=op, fill=fill,
                                             base=base, channel_multiplier=mult))

            select(ident[:, :], [[-1, P]], ALU.not_equal, 1.0, 0, 1)
            nc.gpsimd.memset(rank4[:, 0:1], 1.0).then_inc(consts_made, 1)
            select(ident_h[:, :], [[-1, P]], ALU.not_equal, 1.0, 0, 1)
            select(causal[:, :], [[-1, P]], ALU.is_ge, NEG, 0, 1)
            for r in range(2):
                m = own_mask[:, r, :].rearrange("p (b t) -> p b t", t=DEC_T)
                select(m, [[-32, DEC_B], [-8, DEC_T]], ALU.is_ge, NEG, 128 * r, 1)
                select(m, [[32, DEC_B], [0, DEC_T]], ALU.is_ge, NEG, 31 - 128 * r, -1)
            select(bd_mask[:, :, :], [[-4, DEC_B], [0, DEC_T]], ALU.is_ge, 0.0, 0, 1)
            select(bd_mask[:, :, :], [[4, DEC_B], [0, DEC_T]], ALU.is_ge, 0.0, 3, -1)
            for n in range(1, 4):
                nc.gpsimd.memset(rank4[:, n:n + 1], float(n + 1))
            nc.gpsimd.memset(qbd[:, :, :, :], 0.0).then_inc(consts_made, 1)
            def split_lo(n):
                pool.wait_ge(w_hi_done, split_count(n))
                nc.gpsimd.tensor_tensor(w_split_tile(False, n), w_tile(n), w_split_tile(True, n).bitcast(fp32), ALU.subtract)\
                    .then_inc(w_split["pool"], 1)

            split_lo(0)
            split_lo(1)
            pool.dma_start(wsp[:, :, :], w_spatial[0].rearrange("g t s -> t g s")).then_inc(wsp_in, 16)
            pool.wait_ge(wsp_in, 16)
            nc.gpsimd.affine_select(out=wsp[:, :, :], in_=wsp[:, :, :], pattern=[[0, GRP], [-1, P]],
                                    compare_op=ALU.is_ge, fill=0.0, base=0, channel_multiplier=1)\
                .then_inc(wsp_masked, 1)

            for s in SCHEDULE:
                kind = s[0]
                if kind == "ZE" and ORDER[s[1]][0] in ("q", "k") and s[2] == 1:
                    n = s[1]
                    what, j, _ = ORDER[n]
                    pool.wait_ge(z_free["dve"], freed(Z_FREED_BY, 2 * n + 1)[1])
                    for e in range(2):
                        rows, of = slice(e * HD, (e + 1) * HD), slice(0, HD)
                        lo_rows = slice(HD, P)
                        if what == "q":
                            pool.dma_start(q_st[of, 2 * j + e, :], qk_hi[rows, n % 2, :]).then_inc(staged[n], 16)
                            pool.dma_start(q_st[lo_rows, 2 * j + e, :], qk_lo[rows, n % 2, :]).then_inc(staged[n], 16)
                        else:
                            for half in (of, lo_rows):
                                pool.dma_start(k_hi[half, 2 * j + e, :], qk_hi[rows, n % 2, :]).then_inc(staged[n], 16)
                                pool.dma_start(k_lo[half, 2 * j + e, :], qk_lo[rows, n % 2, :]).then_inc(staged[n], 16)
                elif kind == "Z" and s[2] == 0 and s[1] >= 1 and lo_by(s[1] + 1) == "pool":
                    split_lo(s[1] + 1)
                elif kind == "KVN":
                    tt = s[1]
                    src = kvn[:, tt % 2, :] if tt < 4 else kv_s[:, :]
                    pool.wait_ge(t_free["act"], freed(T_FREED_BY, T_OF[s])[1])
                    landed = stored_kv[tt % 2] if tt < 4 else stored_kvs
                    pool.dma_start(kv_rows(k_prompt, k_sample, tt), src[:, 0:KVW]).then_inc(landed, 16)
                    pool.dma_start(kv_rows(v_prompt, v_sample, tt), src[:, KVW:2 * KVW]).then_inc(landed, 16)
                elif kind == "Z" and s[1:] == (TILE_OF["vs", 2], 0):
                    pool.wait_ge(vst_done, 4)
                    pool.wait_ge(stored_kv[1], 2 * 32)
                    pool.dma_start(g_sgu_bc[:, :], g_sgu[0:1, :].broadcast_to([P, 512])).then_inc(gsgu_in, 16)
                elif kind == "PSC" and s[1] == 0:
                    pool.wait_ge(dpv, 2 * PAGES)
                    for e in range(2):
                        pool.dma_start(b_bc[e * HD:(e + 1) * HD, :, :],
                                       b_spatial[0].rearrange("(o g e) t -> e o g t", e=2, o=1)[e].broadcast_to([HD, 4, P])).then_inc(b_in, 16)
                    pool.dma_start(g_post_bc[:, :], g_post[0:1, :].broadcast_to([P, D])).then_inc(gpost_in, 16)
                elif kind == "LNM":
                    tt = s[1]
                    R = ROWS[tt]
                    n = LNM_N[s]
                    if n == 0:
                        pool.wait_ge(gsgu_in, 16)
                    pool.wait_ge(lnmul_done, n + 1)
                    nc.gpsimd.tensor_tensor(vn[0:R, tt, :], vn[0:R, tt, :], g_sgu_bc[0:R, :], ALU.mult).then_inc(vn_done, 1)
                    if tt == 4:
                        pool.wait_ge(vn_done, n + 1)
                        pool.dma_start(sgu_sample[0].rearrange("b t c -> (b t) c"), vn[0:SMP, 4, :]).then_inc(stored_sgu, 16)
                elif kind == "ZE" and ORDER[s[1]][0] == "gg" and s[2] == 1:
                    j = ORDER[s[1]][1]
                    pool.wait_ge(z_free["dve"], freed(Z_FREED_BY, 2 * s[1] + 1)[1])
                    pool.wait_ge(z_free["act"], freed(Z_FREED_BY, 2 * TILE_OF["u", j] + 1)[1])
                    nc.gpsimd.tensor_tensor(zu[:, j, :], zu[:, j, :], zgg[:, j, :], ALU.mult).then_inc(ug_done, 1)

        @block.scalar
        def _(act):
            chain = [0]

            def link(ins):
                chain[0] += 1
                ins.then_inc(act_chain, 1)
                act.wait_ge(act_chain, chain[0])

            def split_hi(n):
                w_slot_free(act, n)
                if n < 2:
                    act.wait_ge(w_first[n], 16)
                else:
                    act.wait_ge(w_in_s[n // 2 % 2], w_load_count(n))
                nc.scalar.activation(w_split_tile(True, n), w_tile(n), ACT.Copy).then_inc(w_hi_done, 1)

            def x_stats(tt):
                R = ROWS[tt]
                act.wait_ge(x_in[tt], 16)
                link(nc.scalar.activation(x_sq[0:R, :], x_sb[0:R, tt, :], ACT.Square, accum_out=x_ss[0:R, tt:tt + 1]))
                nc.scalar.activation(x_sd[0:R, tt:tt + 1], x_ss[0:R, tt:tt + 1], ACT.Sqrt, scale=1.0 / D, bias=RMS_EPS).then_inc(x_std, 1)

            def take(n, dst, src):
                act.wait_ge(t_full, n + 1)
                nc.scalar.activation(dst, src, ACT.Copy).then_inc(t_free["act"], 1)

            act.wait_ge(consts_made, 1)
            nc.scalar.activation(table_in, rank4[:, 0:1], ACT.Sqrt)

            for s in SCHEDULE:
                kind = s[0]
                if kind == "XT":
                    tt = s[1]
                    R = ROWS[tt]
                    if tt == 0:
                        x_stats(0)
                        x_stats(1)
                    for kk in range(2):
                        act.wait_ge(xt_full, 2 * tt + 2 if tt == 4 else 2 * tt + kk + 1)
                        nc.scalar.activation(act_hi[:, 4 * kk:4 * kk + 4, tokens(tt)],
                                             X_BANK[tt][kk][:, 0:4 * R].rearrange("p (k t) -> p k t", k=4), ACT.Copy).then_inc(x_hi, 1)
                    if tt == 0:
                        split_hi(0)
                    if tt == 1:
                        for later in (2, 3, 4):
                            x_stats(later)
                    if tt == 4:
                        split_hi(1)
                elif kind == "Z":
                    n, half = s[1], s[2]
                    h = 2 * n + half
                    what, j, _ = ORDER[n]
                    if half == 0 and n >= 1:
                        split_hi(n + 1)
                    cols = HALVES[half]
                    wide = cols.stop - cols.start
                    bank, half0 = Z[h % 2], SEQ // 2
                    act.wait_ge(z_full, h + 1)
                    if what in ("q", "k"):
                        if n >= 2:
                            act.wait_ge(staged[n - 2], 64 if n - 2 < 4 else 128)
                        if what == "k":
                            link(nc.scalar.activation(kv32[:, j, cols], bank[:, 0:wide], ACT.Copy))
                        elif half == 1:
                            link(nc.scalar.activation(q_s[:, j, :], bank[:, half0:wide], ACT.Copy, scale=QSCALE))
                        nc.scalar.activation(qk_hi[:, n % 2, half * half0:(half + 1) * half0], bank[:, 0:half0], ACT.Copy,
                                             scale=QSCALE if what == "q" else 1.0).then_inc(z_hi, 1)
                    elif what == "v":
                        nc.scalar.activation(kv32[:, 2 + j, cols], bank[:, 0:wide], ACT.Copy).then_inc(z_free["act"], 1)
                    elif what == "vs":
                        if n == TILE_OF["vs", 0] and half == 0:
                            act.wait_ge(t_full, T_OF["WT",] + 2)
                        nc.scalar.activation(zvs[:, j, cols], bank[:, 0:wide], ACT.Gelu_apprx_tanh).then_inc(z_free["act"], 1)
                    elif what == "u":
                        nc.scalar.activation(zu[:, j, cols], bank[:, 0:wide], ACT.Gelu_apprx_tanh).then_inc(z_free["act"], 1)
                    else:
                        g = GATE_HALVES.index(h)
                        if g >= 2:
                            act.wait_ge(z_free["dve"], freed(Z_FREED_BY, GATE_HALVES[g - 2])[1])
                        nc.scalar.activation(th[:, g % 2, 0:wide], bank[:, 0:wide], ACT.Tanh, scale=0.5).then_inc(z_hi, 1)
                elif kind == "WT":
                    n = T_OF[s]
                    for e in range(2):
                        take(n + e, wspT[:, 4 * e:4 * e + 4, :], T[(n + e) % 2][:, :].rearrange("p (g t) -> p g t", g=4))
                elif kind == "KVN":
                    n, tt = T_OF[s], s[1]
                    R = ROWS[tt]
                    if 2 <= tt < 4:
                        act.wait_ge(stored_kv[tt % 2], 32)
                        act.wait_ge(vst_done, tt - 1)
                    take(n, (kvn[:, tt % 2, :] if tt < 4 else kv_s[:, :]), T[n % 2][0:R, :])
                    if tt < 4:
                        act.wait_ge(t_free["act"], freed(T_FREED_BY, n)[1])
                        nc.scalar.activation(v_st[:, tt, :, 0:HD], kvn[:, tt % 2, KVW:].rearrange("p (h d) -> p h d", h=KVH), ACT.Copy)\
                            .then_inc(vst_hi, 1)
                elif kind == "KTR":
                    _, r, kk, b = s
                    n = T_OF[s]
                    if b == 0 and 2 * r + kk >= 1:
                        act.wait_ge(dsc, 2 * r + kk)
                    take(n, kT[:, 0, b, :], T[n % 2][:, :])
                elif kind == "DEX":
                    r = s[1]
                    act.wait_ge(d_bias, r + 1)
                    if r == 0:
                        act.wait_ge(staged[4], 128)
                        act.wait_ge(staged[5], 128)
                    if r:
                        act.wait_ge(t_full, T_OF["DPT", r - 1] + 3)
                        act.wait_ge(d_rec, r)
                    for blk in range(NBLK):
                        cs = slice(blk * BLOCK, (blk + 1) * BLOCK)
                        nc.scalar.activation(pd[:, cs], S[:, cs], ACT.Exp, bias=bbias[:, blk:blk + 1],
                                             accum_out=dsum[:, blk:blk + 1]).then_inc(act_chain, 1)
                        chain[0] += 1
                    nc.scalar.activation(p_own[:, :], own_s[:, :], ACT.Exp, bias=nm_d, accum_out=dsum[:, 4:5]).then_inc(d_exp, 1)
                elif kind == "DPT":
                    r, n = s[1], T_OF[s]
                    if r:
                        act.wait_ge(dpv, PAGES * r)
                    take(n, pdT[:, 0:4, :], T[n % 2][:, :].rearrange("p (j q) -> p j q", j=4))
                    take(n + 2, p_ownT[:, :], T[(n + 2) % 2][0:SMP, 0:P])
                elif kind == "VSN":
                    tt = s[1]
                    R = ROWS[tt]
                    act.wait_ge(t_free["dve"], freed(T_FREED_BY, T_OF[s])[1])
                    if tt:
                        act.wait_ge(ssq_done, tt)
                    else:
                        act.wait_ge(stored_kv[0], 2 * 32)
                    nc.scalar.activation(ln_sq[0:R, :], vn[0:R, tt, :], ACT.Square).then_inc(sq_done, 1)
                elif kind == "LN":
                    act.wait_ge(ssq_done, TT)
                    nc.scalar.activation(ln_std[:, 0:4, :], ln_var[:, 0:4, :], ACT.Sqrt, scale=1.0 / GCH, bias=LN_EPS).then_inc(lnstd_done, 1)
                    nc.scalar.activation(ln_std[0:SMP, 4, :], ln_var[0:SMP, 4, :], ACT.Sqrt, scale=1.0 / GCH, bias=LN_EPS).then_inc(lnstd_done, 1)
                elif kind == "PSC":
                    u = s[1]
                    keys = P * (UNITS[u][1] + 1)
                    if u == 0:
                        act.wait_ge(dsc, 4)
                    if u >= 2:
                        act.wait_ge(t_full, T_OF["PTR", u - 2] + 2)
                        act.wait_ge(p_norm, 2 * u - 2)
                    for g in range(2):
                        act.wait_ge(p_max, 2 * u + g + 1)
                        ins = nc.scalar.activation(probs[:, u % 2, g, 0:keys], S[:, g * 512:g * 512 + keys], ACT.Exp,
                                                   bias=nmax[:, u % 2, g:g + 1], accum_out=psums[:, u % 2, g:g + 1])
                        ins.then_inc(p_exp, 1)
                elif kind == "PTR":
                    u, n = s[1], T_OF[s]
                    blocks = UNITS[u][1] + 1
                    if u == 0:
                        act.wait_ge(dsc, 4)
                    if u >= 2:
                        act.wait_ge(ppv, u - 1)
                    for g in range(2):
                        act.wait_ge(t_full, n + g + 1)
                        nc.scalar.activation(pT_hi[:, u % 2, 0:blocks, g, :],
                                             T[(n + g) % 2][:, 0:blocks * P].rearrange("p (j q) -> p j q", q=P), ACT.Copy)\
                            .then_inc(pT_hi_done, 1)
                elif kind == "ATT":
                    u = s[1]
                    act.wait_ge(ppv, u + 1)
                    if u >= 2:
                        act.wait_ge(att_done, u - 1)
                    nc.scalar.activation(o_tmp[:, u % 2, :], O[u % 2][HD:P, 0:256], ACT.Copy).then_inc(o_hi, 1)
                elif kind == "MIX":
                    k, half = s[1], s[2]
                    mix_ready(act, k, half)
                    nc.scalar.activation(act_hi[:, k, MIX_COLS[half]], mixed(k, MIX_COLS[half]), ACT.Copy).then_inc(mix_hi, 1)
                elif kind == "YF":
                    hf = s[1]
                    act.wait_ge(ys, 2 * (hf + 1))
                    if hf:
                        act.wait_ge(y_fold, 1)
                    for g in range(1, 4):
                        nc.scalar.activation(y_part[:, g - 1, :], Y[hf][4][g * SMP:(g + 1) * SMP, :], ACT.Copy).then_inc(y_parts, 1)
                elif kind in ("Y", "YS", "YH", "Y2"):
                    for c in OUT_SPLITS.get(s, []):
                        split_hi(NT + c)

                    def squares(hf, tt):
                        n = TT * hf + (tt if hf == 0 else Y_ORDER.index(tt))
                        if tt < 4:
                            act.wait_ge(y_full, 4 * (4 if hf else 3) + tt + 1)
                        else:
                            act.wait_ge(y_fold, hf + 1)
                        if n:
                            act.wait_ge(y_sq, n)
                        R = ROWS[tt]
                        nc.scalar.activation(ln_sq[0:R, :], y_src(hf, tt), ACT.Square,
                                             accum_out=y_ss[0:R, 5 * hf + tt:5 * hf + tt + 1]).then_inc(y_sq, 1)
                        return n + 1

                    if kind == "YH":
                        for tt in range(TT):
                            squares(0, tt)
                    elif kind == "Y2":
                        tt = s[1]
                        R = ROWS[tt]
                        act.wait_ge(y_sq, squares(1, tt))
                        act.wait_ge(y_bias, 1)
                        nc.scalar.activation(y_sd[0:R, tt:tt + 1], y_ss[0:R, 5 + tt:6 + tt], ACT.Sqrt, scale=1.0 / D,
                                             bias=y_b[0:R, tt:tt + 1]).then_inc(y_std, 1)

        @block.vector
        def _(dve):
            chain = [0]

            def link(ins):
                chain[0] += 1
                ins.then_inc(dve_chain, 1)
                dve.wait_ge(dve_chain, chain[0])

            def split_lo(n):
                dve.wait_ge(w_hi_done, split_count(n))
                nc.vector.tensor_tensor(w_split_tile(False, n), w_tile(n), w_split_tile(True, n).bitcast(fp32), ALU.subtract)\
                    .then_inc(w_split["dve"], 1)

            def x_norm(tt):
                R = ROWS[tt]
                dve.wait_ge(x_std, tt + 1)
                link(nc.vector.reciprocal(x_rs[0:R, tt:tt + 1], x_sd[0:R, tt:tt + 1]))
                if tt >= 3:
                    dve.wait_ge(xt_full, 2 * tt - 4)
                for kk in range(2):
                    cs = slice(kk * 512, (kk + 1) * 512)
                    nc.vector.scalar_tensor_tensor(xn[0:R, tt % 3, cs], x_sb[0:R, tt, cs], x_rs[0:R, tt:tt + 1], g_pre_bc[0:R, cs],
                                                   ALU.mult, ALU.mult).then_inc(xn_done, 1)

            for s in SCHEDULE:
                kind = s[0]
                if kind == "XT":
                    tt = s[1]
                    R = ROWS[tt]
                    if tt == 0:
                        dve.wait_ge(gpre_in, 16)
                        x_norm(0)
                        x_norm(1)
                    for kk in range(2):
                        dve.wait_ge(x_hi, 2 * tt + 2 if tt == 4 else 2 * tt + kk + 1)
                        nc.vector.tensor_tensor(act_lo[:, 4 * kk:4 * kk + 4, tokens(tt)],
                                                X_BANK[tt][kk][:, 0:4 * R].rearrange("p (k t) -> p k t", k=4),
                                                act_hi[:, 4 * kk:4 * kk + 4, tokens(tt)].bitcast(fp32), ALU.subtract)\
                            .then_inc(x_split, 1)
                    if tt == 1:
                        for later in (2, 3, 4):
                            x_norm(later)
                elif kind == "Z":
                    if s[2] == 0 and s[1] >= 1 and lo_by(s[1] + 1) == "dve":
                        split_lo(s[1] + 1)
                elif kind == "ZE":
                    n, half = s[1], s[2]
                    h = 2 * n + half
                    what, j, _ = ORDER[n]
                    cols = HALVES[half]
                    wide = cols.stop - cols.start
                    bank, half0 = Z[h % 2], SEQ // 2
                    if what in ("q", "k"):
                        cs = slice(half * half0, (half + 1) * half0)
                        dve.wait_ge(z_hi, h + 1)
                        ins = nc.vector.scalar_tensor_tensor(qk_lo[:, n % 2, cs], bank[:, 0:half0], QSCALE if what == "q" else 1.0,
                                                             qk_hi[:, n % 2, cs].bitcast(fp32), ALU.mult, ALU.subtract)
                        ins.then_inc(z_free["dve"], 1)
                        if n == 3 and half == 1:
                            dve.wait_ge(consts_made, 2)
                            view = qbd[:, :, :, :].rearrange("p c r (x h) -> p c r x h", h=HEADS)
                            for hd in range(HEADS):
                                kvh, g = hd // 2, hd % 2
                                to = (kvh % 2) * HD
                                ins = nc.vector.tensor_copy(view[to:to + HD, kvh // 2, :, :, hd],
                                                            q_s[g * HD:(g + 1) * HD, kvh, :].rearrange("p (r x) -> p r x", r=2))
                            ins.then_inc(qbd_done, 1)
                    elif what in ("ga", "gg"):
                        g = GATE_HALVES.index(h)
                        dst = zga if what == "ga" else zgg
                        dve.wait_ge(z_hi, 12 + g + 1)
                        if g == 0:
                            dve.wait_ge(t_full, T_OF["VSN", 4] + 1)
                        if what == "gg" and j == 0 and half == 0:
                            dve.wait_ge(t_full, T_OF["KVN", 3] + 1)
                            dve.wait_ge(down, 2)
                        nc.vector.scalar_tensor_tensor(dst[:, j, cols], th[:, g % 2, 0:wide], 1.0, bank[:, 0:wide], ALU.add, ALU.mult)\
                            .then_inc(z_free["dve"], 1)
                elif kind == "WT":
                    dve.wait_ge(consts_made, 2)
                    nc.vector.tensor_copy(rep4[:, :].rearrange("p (b t) -> p b t", t=DEC_T),
                                          ident[0:DEC_T, 0:DEC_T].unsqueeze(1).broadcast_to([DEC_T, DEC_B, DEC_T])).then_inc(rep_done, 1)
                elif kind == "WB":
                    n = T_OF[s]
                    dve.wait_ge(t_full, n + 1)
                    nc.vector.tensor_tensor(w_bd[:, :, :].rearrange("p g (b t) -> p g b t", t=DEC_T),
                                            T[n % 2][0:SMP, 0:GRP * DEC_T].rearrange("p (g t) -> p g t", g=GRP).unsqueeze(2).broadcast_to([SMP, GRP, DEC_B, DEC_T]),
                                            bd_mask[:, :, :].unsqueeze(1).broadcast_to([SMP, GRP, DEC_B, DEC_T]), ALU.mult)\
                        .then_inc(t_free["dve"], 1)
                elif kind == "KVN":
                    tt = s[1]
                    if tt < 4:
                        dve.wait_ge(vst_hi, tt + 1)
                        nc.vector.tensor_tensor(v_st[:, tt, :, HD:], kvn[:, tt % 2, KVW:].rearrange("p (h d) -> p h d", h=KVH),
                                                v_st[:, tt, :, 0:HD].bitcast(fp32), ALU.subtract).then_inc(vst_done, 1)
                elif kind == "KTR":
                    _, r, kk, b = s
                    n = T_OF[s] + 1
                    if b == 0 and 2 * r + kk >= 1:
                        dve.wait_ge(dsc, 2 * r + kk)
                    dve.wait_ge(t_full, n + 1)
                    nc.vector.tensor_copy(kT[:, 1, b, :], T[n % 2][:, :]).then_inc(t_free["dve"], 1)
                elif kind == "DOWN":
                    r = s[1]
                    dve.wait_ge(down, r + 1)
                    if r:
                        dve.wait_ge(d_exp, r)
                    link(nc.vector.tensor_tensor(own_s[:, :], O[0][:, 0:SMP], own_mask[:, r, :], ALU.add))
                elif kind == "DSM":
                    r = s[1]
                    dve.wait_ge(dsc, 2 * r + 2)
                    if r:
                        dve.wait_ge(d_exp, r)
                    blocks = S[:, :].rearrange("p (n c) -> p n c", n=NBLK)
                    nc.vector.tensor_reduce(gsum, blocks, AX.X, ALU.add).then_inc(dve_chain, 1)
                    nc.vector.tensor_reduce(bmax, blocks, AX.X, ALU.max).then_inc(dve_chain, 1)
                    chain[0] += 2
                    link(nc.vector.tensor_reduce(omax, own_s[:, :], AX.X, ALU.max))
                    link(nc.vector.tensor_reduce(gmin, gsum, AX.X, ALU.min))
                    link(nc.vector.scalar_tensor_tensor(wdrop, gsum, gmin, rank4[:, :], ALU.is_equal, ALU.mult))
                    link(nc.vector.tensor_reduce(wmax, wdrop, AX.X, ALU.max))
                    link(nc.vector.tensor_scalar(drop, wdrop, wmax, NEG, ALU.is_equal, ALU.mult))
                    link(nc.vector.tensor_tensor(bmsk, bmax, drop, ALU.add))
                    link(nc.vector.tensor_reduce(tmax, bmsk, AX.X, ALU.max))
                    link(nc.vector.tensor_scalar(nm_d, tmax, omax, -1.0, ALU.max, ALU.mult))
                    nc.vector.tensor_scalar(bbias, drop, nm_d, None, ALU.add).then_inc(d_bias, 1)
                elif kind == "DEX":
                    r = s[1]
                    dve.wait_ge(d_exp, r + 1)
                    link(nc.vector.tensor_reduce(dtot, dsum, AX.X, ALU.add))
                    nc.vector.reciprocal(drec[r], dtot).then_inc(d_rec, 1)
                elif kind == "DPT":
                    n = T_OF[s] + 1
                    if s[1]:
                        dve.wait_ge(dpv, PAGES)
                    dve.wait_ge(t_full, n + 1)
                    nc.vector.tensor_copy(pdT[:, 4:8, :], T[n % 2][:, :].rearrange("p (j q) -> p j q", j=4)).then_inc(t_free["dve"], 1)
                elif kind == "DOD":
                    r = s[1]
                    dve.wait_ge(dpv, PAGES * (r + 1))
                    if r:
                        dve.wait_ge(t_full, T_OF["DOT", 0] + 1)
                    dve.wait_ge(d_rec, r + 1)
                    nc.vector.tensor_scalar(od[:, :], O[1][:, 0:KVW], drec[r], 0.5, ALU.mult, ALU.mult).then_inc(od_done, 1)
                elif kind == "DOT":
                    r, n = s[1], T_OF[s]
                    dve.wait_ge(t_full, n + 1)
                    for hd in range(HEADS):
                        kvh, g = hd // 2, hd % 2
                        frm = (kvh % 2) * HD
                        src = T[n % 2][frm:frm + HD, (kvh // 2) * P:(kvh // 2 + 1) * P].rearrange("p (x h) -> p x h", h=HEADS)[:, :, hd]
                        ins = nc.vector.tensor_copy(att_s[g * HD:(g + 1) * HD, kvh, 16 * r:16 * r + 16], src)
                        ins.then_inc(t_free["dve"] if hd == HEADS - 1 else dve_chain, 1)
                    chain[0] += HEADS - 1
                elif kind == "VSN":
                    tt, n = s[1], T_OF[s]
                    R = ROWS[tt]
                    src = T[n % 2][0:R, :].rearrange("p (g c) -> p g c", g=GRP)
                    dve.wait_ge(t_full, n + 1)
                    link(nc.vector.tensor_reduce(ln_mu[0:R, 0, :], src, AX.X, ALU.add))
                    link(nc.vector.tensor_scalar(ln_mu[0:R, 1, :], ln_mu[0:R, 0, :], 1.0 / GCH, None, ALU.mult))
                    vt = vn[0:R, tt, :].rearrange("p (g c) -> p g c", g=GRP)
                    nc.vector.tensor_tensor(vt, src, ln_mu[0:R, 1, :].unsqueeze(2).broadcast_to([R, GRP, GCH]), ALU.subtract).then_inc(t_free["dve"], 1)
                    dve.wait_ge(sq_done, tt + 1)
                    nc.vector.tensor_reduce(ln_var[0:R, tt, :], ln_sq[0:R, :].rearrange("p (g c) -> p g c", g=GRP), AX.X, ALU.add).then_inc(ssq_done, 1)
                elif kind == "LN":
                    dve.wait_ge(lnstd_done, 2)
                    nc.vector.reciprocal(ln_rstd[:, 0:4, :], ln_std[:, 0:4, :]).then_inc(dve_chain, 1)
                    chain[0] += 1
                    link(nc.vector.reciprocal(ln_rstd[0:SMP, 4, :], ln_std[0:SMP, 4, :]))
                elif kind == "LNM":
                    tt = s[1]
                    R = ROWS[tt]
                    vt = vn[0:R, tt, :].rearrange("p (g c) -> p g c", g=GRP)
                    nc.vector.tensor_tensor(vt, vt, ln_rstd[0:R, tt, :].unsqueeze(2).broadcast_to([R, GRP, GCH]), ALU.mult).then_inc(lnmul_done, 1)
                elif kind == "PSC":
                    u = s[1]
                    keys = P * (UNITS[u][1] + 1)
                    if u >= 2:
                        dve.wait_ge(p_exp, 2 * u - 2)
                    for g in range(2):
                        dve.wait_ge(psc, 2 * u + g + 1)
                        nc.vector.tensor_reduce(nmax[:, u % 2, g:g + 1], S[:, g * 512:g * 512 + keys], AX.X, ALU.max, negate=True)\
                            .then_inc(p_max, 1)
                elif kind == "PN":
                    u = s[1]
                    keys = P * (UNITS[u][1] + 1)
                    for g in range(2):
                        dve.wait_ge(p_exp, 2 * u + g + 1)
                        link(nc.vector.reciprocal(rsum[:, u % 2, g:g + 1], psums[:, u % 2, g:g + 1]))
                        part = probs[:, u % 2, g, 0:keys]
                        nc.vector.tensor_scalar(part, part, rsum[:, u % 2, g:g + 1], 0.5, ALU.mult, ALU.mult).then_inc(p_norm, 1)
                elif kind == "PTR":
                    u, n = s[1], T_OF[s]
                    blocks = UNITS[u][1] + 1
                    for g in range(2):
                        dve.wait_ge(pT_hi_done, 2 * u + g + 1)
                        nc.vector.tensor_tensor(pT_lo[:, u % 2, 0:blocks, g, :],
                                                T[(n + g) % 2][:, 0:blocks * P].rearrange("p (j q) -> p j q", q=P),
                                                pT_hi[:, u % 2, 0:blocks, g, :].bitcast(fp32), ALU.subtract)\
                            .then_inc(t_free["dve"], 1)
                elif kind == "ATT":
                    u = s[1]
                    kvh, i = UNITS[u]
                    dve.wait_ge(o_hi, u + 1)
                    for g in range(2):
                        link(nc.vector.tensor_tensor(att[g * HD:(g + 1) * HD, u % 2, :], O[u % 2][0:HD, g * P:(g + 1) * P],
                                                     o_tmp[:, u % 2, g * P:(g + 1) * P], ALU.add))
                    dve.wait_ge(z_free["dve"], freed(Z_FREED_BY, 2 * TILE_OF["ga", kvh] + i // 2)[1])
                    part = zga[:, kvh, i * P:(i + 1) * P]
                    nc.vector.tensor_tensor(part, part, att[:, u % 2, :], ALU.mult).then_inc(att_done, 1)
                elif kind == "SP":
                    gp, n = s[1], T_OF[s]
                    dve.wait_ge(t_full, n + 1)
                    dve.wait_ge(b_in, 32)
                    if gp:
                        dve.wait_ge(sp_done, gp)
                    nc.vector.tensor_tensor(sp_sum[:, :].rearrange("p (c t) -> p c t", t=P), T[n % 2][:, :].rearrange("p (c t) -> p c t", t=P),
                                                 b_bc[:, gp, :].unsqueeze(1).broadcast_to([P, 4, P]), ALU.add).then_inc(t_free["dve"], 1)
                    dve.wait_ge(t_free["dve"], freed(T_FREED_BY, n)[1])
                    dve.wait_ge(ug_done, gp + 1)
                    nc.vector.scalar_tensor_tensor(zgg[:, gp, 0:SEQ], sp_sum[:, :], 0.5, zu[:, gp, 0:SEQ], ALU.mult, ALU.mult).then_inc(sp_done, 1)
                elif kind == "SPS":
                    n = T_OF[s]
                    dve.wait_ge(t_full, n + 1)
                    dve.wait_ge(ug_done, 4)
                    src = T[n % 2][:, 0:4 * SMP].rearrange("p (g b t) -> p g b t", g=4, t=DEC_T)
                    tmp = sp_sum[:, 0:4 * SMP].rearrange("p (g b t) -> p g b t", g=4, t=DEC_T)
                    dve.wait_ge(sp_done, 4)
                    nc.vector.tensor_tensor(tmp, src, b_bc[:, :, 0:DEC_T].unsqueeze(2).broadcast_to([P, 4, DEC_B, DEC_T]), ALU.add)\
                        .then_inc(t_free["dve"], 1)
                    dve.wait_ge(t_free["dve"], freed(T_FREED_BY, n)[1])
                    nc.vector.scalar_tensor_tensor(zgg[:, :, SEQ:TOK], sp_sum[:, 0:4 * SMP].rearrange("p (g x) -> p g x", g=4), 0.5,
                                                   zu[:, :, SEQ:TOK], ALU.mult, ALU.mult).then_inc(sp_done, 1)
                elif kind == "AS":
                    dve.wait_ge(z_free["dve"], freed(Z_FREED_BY, 2 * TILE_OF["ga", 3] + 1)[1])
                    dve.wait_ge(t_free["dve"], freed(T_FREED_BY, T_OF["DOT", 1])[1])
                    nc.vector.tensor_tensor(zga[:, :, SEQ:TOK], zga[:, :, SEQ:TOK], att_s[:, :, :], ALU.mult).then_inc(as_done, 1)
                elif kind == "MIX":
                    k, cs = s[1], MIX_COLS[s[2]]
                    dve.wait_ge(mix_hi, MIX_N[s] + 1)
                    nc.vector.tensor_tensor(act_lo[:, k, cs], mixed(k, cs),
                                            act_hi[:, k, cs].bitcast(fp32), ALU.subtract).then_inc(mix_done, 1)
                elif kind == "YF":
                    hf = s[1]
                    total = y_sum[:, hf, :]
                    dve.wait_ge(y_parts, 3 * (hf + 1))
                    link(nc.vector.tensor_tensor(total, y_part[:, 0, :], y_part[:, 1, :], ALU.add))
                    link(nc.vector.tensor_tensor(total, total, y_part[:, 2, :], ALU.add))
                    nc.vector.tensor_tensor(total, total, Y[hf][4][0:SMP, :], ALU.add).then_inc(y_fold, 1)
                elif kind in ("Y", "YS", "YH", "Y2"):
                    for c in OUT_SPLITS.get(s, []):
                        split_lo(NT + c)

                    def scaled(hf, tt, n):
                        R = ROWS[tt]
                        cs = slice(hf * 512, (hf + 1) * 512)
                        dve.wait_ge(y_sq, n + 1)
                        nc.vector.tensor_tensor(y_sb[0:R, tt, cs], y_src(hf, tt), g_post_bc[0:R, cs], ALU.mult).then_inc(y_out, 1)

                    if kind == "YH":
                        dve.wait_ge(ppv, len(UNITS))
                        dve.wait_ge(gpost_in, 16)
                        for tt in range(TT):
                            scaled(0, tt, tt)
                        nc.vector.tensor_scalar(y_b[:, 0:4], y_ss[:, 0:4], 1.0 / D, RMS_EPS, ALU.mult, ALU.add).then_inc(dve_chain, 1)
                        chain[0] += 1
                        dve.wait_ge(dve_chain, chain[0])
                        nc.vector.tensor_scalar(y_b[0:SMP, 4:5], y_ss[0:SMP, 4:5], 1.0 / D, RMS_EPS, ALU.mult, ALU.add).then_inc(y_bias, 1)
                    elif kind == "Y2":
                        tt = s[1]
                        n = TT + Y_ORDER.index(tt)
                        R = ROWS[tt]
                        scaled(1, tt, n)
                        dve.wait_ge(y_std, n - TT + 1)
                        link(nc.vector.reciprocal(y_rs[0:R, tt:tt + 1], y_sd[0:R, tt:tt + 1]))
                        dve.wait_ge(xr_in[tt], 16)
                        for hf in range(2):
                            cs = slice(hf * 512, (hf + 1) * 512)
                            dve.wait_ge(y_out, n + 1 if hf else tt + 1)
                            nc.vector.scalar_tensor_tensor(y_sb[0:R, tt, cs], y_sb[0:R, tt, cs], y_rs[0:R, tt:tt + 1],
                                                           x_res[0:R, tt, cs], ALU.mult, ALU.add).then_inc(y_done, 1)

        @block.tensor
        def _(pe):
            mm = nc.tensor.matmul

            def turn(n, col, in_, rows, out_rows):
                return nc.tensor.transpose(T[n % 2][0:out_rows, col:col + rows], in_, ident[0:rows, 0:rows])

            def ktr_in(m):
                pe.wait_ge(k_in[m % 4], 64 * (m // 4 + 1))

            pe.wait_ge(consts_made, 1)

            def turn_x(tt):
                R = ROWS[tt]
                if tt == 3:
                    pe.wait_ge(x_split, 2)
                for kk in range(2):
                    pe.wait_ge(xn_done, 2 * tt + kk + 1)
                    for k in range(4):
                        last = nc.tensor.transpose(X_BANK[tt][kk][:, k * R:(k + 1) * R],
                                                   xn[0:R, tt % 3, (4 * kk + k) * P:(4 * kk + k + 1) * P], ident[0:R, 0:R])
                    last.then_inc(xt_full, 1)

            def project(hf, tt, kp, first, end):
                R = ROWS[tt]
                for e in range(2):
                    k = 2 * kp + e
                    wh, wl = (w_split_tile(hi, NT + 4 * hf + kp)[:, e * 512:(e + 1) * 512] for hi in (True, False))
                    mm(Y[hf][tt][0:R, :], act_hi[:, k, tokens(tt)], wh, start=(first and e == 0), stop=False)
                    mm(Y[hf][tt][0:R, :], act_lo[:, k, tokens(tt)], wh, start=False, stop=False)
                    last = mm(Y[hf][tt][0:R, :], act_hi[:, k, tokens(tt)], wl, start=False, stop=(end and e == 1))
                return last

            for s in SCHEDULE:
                kind, n = s[0], T_OF[s]
                if kind == "XT":
                    if s[1] < 2:
                        turn_x(s[1])
                elif kind == "Z":
                    t, half = s[1], s[2]
                    h = 2 * t + half
                    if t == 0:
                        pe.wait_ge(x_split, 4 if half == 0 else 2 * TT)
                    if half == 0:
                        pe.wait_ge(w_split[lo_by(t)], lo_count(t))
                    z_bank_free(pe, h)
                    cols = HALVES[half]
                    out = Z[h % 2][:, 0:cols.stop - cols.start]
                    wh, wl = w_split_tile(True, t), w_split_tile(False, t)
                    for k in range(KD):
                        mm(out, wh[:, k, :], act_hi[:, k, cols], start=(k == 0), stop=False)
                        mm(out, wh[:, k, :], act_lo[:, k, cols], start=False, stop=False)
                        last = mm(out, wl[:, k, :], act_hi[:, k, cols], start=False, stop=(k == KD - 1))
                        if h == 0 and k in (1, 3, 5):
                            turn_x(2 + k // 2)
                    last.then_inc(z_full, 1)
                elif kind == "WT":
                    pe.wait_ge(wsp_masked, 1)
                    for e in range(2):
                        bank_free(pe, n + e)
                        for g in range(4):
                            last = turn(n + e, g * P, wsp[:, 4 * e + g, :], P, P)
                        last.then_inc(t_full, 1)
                elif kind == "WB":
                    bank_free(pe, n)
                    pe.wait_ge(rep_done, 1)
                    by, count = freed(T_FREED_BY, T_OF["WT",] + 1)
                    pe.wait_ge(t_free[by], count)
                    mm(T[n % 2][0:SMP, 0:GRP * DEC_T], rep4[:, :], wspT[0:DEC_T, :, 0:DEC_T], start=True, stop=True).then_inc(t_full, 1)
                elif kind == "KVN":
                    tt = s[1]
                    bank_free(pe, n)
                    if tt == 0:
                        pe.wait_ge(z_free["act"], freed(Z_FREED_BY, 2 * TILE_OF["v", 1] + 1)[1])
                        pe.wait_ge(z_hi, 12)
                    for j in range(4):
                        last = turn(n, j * P, kv32[:, j, tokens(tt)], P, ROWS[tt])
                    last.then_inc(t_full, 1)
                elif kind == "KTR":
                    _, r, kk, b = s
                    ktr_in(KTR_N[s])
                    for c in range(2):
                        bank_free(pe, n + c)
                        for j in range(4):
                            last = turn(n + c, j * P, k_slot(KTR_N[s])[:, j, c * P:(c + 1) * P], P, P)
                        last.then_inc(t_full, 1)
                elif kind == "DSC":
                    r, kk = s[1], s[2]
                    if r == 0 and kk == 0:
                        pe.wait_ge(qbd_done, 1)
                    for e in range(2):
                        by, count = freed(T_FREED_BY, T_OF["KTR", r, kk, 3] + e)
                        pe.wait_ge(t_free[by], count)
                    if r:
                        pe.wait_ge(d_exp, r)
                    for c in range(2):
                        for b in range(4):
                            last = mm(S[32 * b:32 * b + 32, kk * 512:(kk + 1) * 512], qbd[:, c, r, 32 * b:32 * b + 32], kT[:, c, b, :],
                                      start=(c == 0), stop=(c == 1))
                    last.then_inc(dsc, 1)
                elif kind == "DOWN":
                    r = s[1]
                    pe.wait_ge(z_hi, 12)
                    if r:
                        pe.wait_ge(d_bias, r)
                    for c in range(2):
                        last = mm(O[0][:, 0:SMP], qbd[:, c, r, :], kv32[:, c, SEQ:TOK], start=(c == 0), stop=(c == 1))
                    last.then_inc(down, 1)
                elif kind == "DPT":
                    r = s[1]
                    pe.wait_ge(d_exp, r + 1)
                    for e in range(2):
                        bank_free(pe, n + e)
                        for j in range(4):
                            last = turn(n + e, j * P, pd[:, (4 * e + j) * P:(4 * e + j + 1) * P], P, P)
                        last.then_inc(t_full, 1)
                    bank_free(pe, n + 2)
                    nc.tensor.transpose(T[(n + 2) % 2][0:SMP, 0:P], p_own[:, :], ident[:, :]).then_inc(t_full, 1)
                elif kind == "DPV":
                    r, pg = s[1], s[2]
                    m = r * PAGES + pg
                    if pg == 0:
                        for e in range(2):
                            by, count = freed(T_FREED_BY, T_OF["DPT", r] + e)
                            pe.wait_ge(t_free[by], count)
                        if r:
                            pe.wait_ge(od_done, r)
                    pe.wait_ge(v_in[m % 4], 64 * (m // 4 + 1))
                    for b in range(4):
                        last = mm(O[1][32 * b:32 * b + 32, 0:KVW], pdT[:, pg, 32 * b:32 * b + 32], v_ring[:, m % 4, b, :],
                                  start=(pg == 0), stop=False, skip_group_check=True)
                    if pg == PAGES - 1:
                        for use in (T_OF["DPT", r] + 2, T_OF["KVN", 4]):
                            by, count = freed(T_FREED_BY, use)
                            pe.wait_ge(t_free[by], count)
                        last = mm(O[1][:, 0:KVW], p_ownT[:, :], kv_s[:, KVW:2 * KVW], start=False, stop=True, skip_group_check=True)
                    last.then_inc(dpv, 1)
                elif kind == "DOT":
                    r = s[1]
                    bank_free(pe, n)
                    pe.wait_ge(od_done, r + 1)
                    for c in range(2):
                        last = turn(n, c * P, od[:, c * P:(c + 1) * P], P, P)
                    last.then_inc(t_full, 1)
                elif kind == "VSN":
                    tt = s[1]
                    bank_free(pe, n)
                    if tt == 0:
                        pe.wait_ge(z_free["act"], freed(Z_FREED_BY, 2 * TILE_OF["vs", 3] + 1)[1])
                    for j in range(4):
                        last = turn(n, j * P, zvs[:, j, tokens(tt)], P, ROWS[tt])
                    last.then_inc(t_full, 1)
                elif kind == "PSC":
                    u = s[1]
                    kvh, i = UNITS[u]
                    if i == 0:
                        pe.wait_ge(staged[kvh], 64)
                        pe.wait_ge(staged[4 + kvh // 2], 128)
                    if u == 0:
                        pe.wait_ge(d_exp, 2)
                    keys = max(2 * P, P * (i + 1))
                    for g in range(2):
                        if u:
                            pe.wait_ge(p_exp, 2 * u - 1 + g)
                        out = S[:, g * 512:g * 512 + keys]
                        q = q_st[:, 2 * kvh + g, i * P:(i + 1) * P]
                        mm(out, q, k_hi[:, kvh, 0:keys], start=True, stop=False)
                        mm(S[:, g * 512 + i * P:g * 512 + (i + 1) * P], ident_h[:, :], causal[:, :], start=False, stop=False, skip_group_check=True)
                        mm(out, q, k_lo[:, kvh, 0:keys], start=False, stop=True).then_inc(psc, 1)
                elif kind == "PTR":
                    u = s[1]
                    for g in range(2):
                        pe.wait_ge(p_norm, 2 * u + g + 1)
                        bank_free(pe, n + g)
                        for j in range(UNITS[u][1] + 1):
                            last = turn(n + g, j * P, probs[:, u % 2, g, j * P:(j + 1) * P], P, P)
                        last.then_inc(t_full, 1)
                elif kind == "PPV":
                    u = s[1]
                    kvh, i = UNITS[u]
                    by, count = freed(T_FREED_BY, T_OF["PTR", u] + 1)
                    pe.wait_ge(t_free[by], count)
                    if u == 0:
                        pe.wait_ge(vst_done, 4)
                        pe.wait_ge(d_bias, 2)
                    elif u == 1:
                        pe.wait_ge(od_done, 2)
                    else:
                        pe.wait_ge(att_done, u - 1)
                    for j in range(i + 1):
                        for e, part in enumerate((pT_hi, pT_lo)):
                            last = mm(O[u % 2][:, 0:256], v_st[:, j, kvh, :], part[:, u % 2, j, :, :].rearrange("p g q -> p (g q)"),
                                      start=(j == 0 and e == 0), stop=(j == i and e == 1))
                    last.then_inc(ppv, 1)
                elif kind == "SP":
                    gp = s[1]
                    bank_free(pe, n)
                    pe.wait_ge(vn_done, TT)
                    for c in range(4):
                        for e in range(2):
                            g = 2 * gp + e
                            last = mm(T[n % 2][e * HD:(e + 1) * HD, c * P:(c + 1) * P], vn[:, c, g * GCH:(g + 1) * GCH], wspT[:, g, :], start=True, stop=True)
                    last.then_inc(t_full, 1)
                elif kind == "SPS":
                    bank_free(pe, n)
                    pe.wait_ge(t_free["dve"], freed(T_FREED_BY, T_OF["WB",])[1])
                    for g in range(GRP):
                        e, gp = g % 2, g // 2
                        last = mm(T[n % 2][e * HD:(e + 1) * HD, gp * SMP:(gp + 1) * SMP], vn[0:SMP, 4, g * GCH:(g + 1) * GCH], w_bd[:, g, :], start=True, stop=True)
                    last.then_inc(t_full, 1)
                elif kind == "YS":
                    p = s[1]
                    hf, m = p // 2, NT // 2 + p
                    pe.wait_ge(w_in_s[m % 2], w_load_count(2 * m))
                    if p == 0:
                        pe.wait_ge(as_done, 1)
                        pe.wait_ge(att_done, len(UNITS) - 1)
                    elif p == 1:
                        pe.wait_ge(sp_done, 5)
                    elif p == 2:
                        by, count = freed(T_FREED_BY, [n for n in range(len(T_FREED_BY)) if n % 2 == 0][-1])
                        pe.wait_ge(t_free[by], count)
                    for g in range(4):
                        last = mm(Y[hf][4][g * SMP:(g + 1) * SMP, :], mixed(4 * (p % 2) + g, slice(SEQ, TOK)),
                                  w_raw[:, m % 2, g * 512:(g + 1) * 512], start=(p % 2 == 0), stop=(p % 2 == 1))
                    last.then_inc(ys, 1)
                elif kind == "Y":
                    c = s[1]
                    pe.wait_ge(w_split[lo_by(NT + c)], lo_count(NT + c))
                    if c == 0:
                        pe.wait_ge(z_free["dve"], freed(Z_FREED_BY, 2 * NT - 1)[1])
                        pe.wait_ge(p_exp, 2 * len(UNITS))
                    for tt in range(4):
                        for e in range(2):
                            pe.wait_ge(mix_done, MIX_N["MIX", 2 * c + e, tt // 2] + 1)
                        last = project(0, tt, c, c == 0, c == 3)
                        last.then_inc(y_full, 1)
                elif kind == "Y2" and s[1] < 4:
                    tt = s[1]
                    if tt == 0:
                        for use in (len(T_FREED_BY) - 2, len(T_FREED_BY) - 1):
                            by, count = freed(T_FREED_BY, use)
                            pe.wait_ge(t_free[by], count)
                        pe.wait_ge(att_done, len(UNITS))
                    if tt == 2:
                        pe.wait_ge(y_out, 2)
                    for c in range(4):
                        if tt == 0:
                            pe.wait_ge(w_split["dve"], lo_count(NT + 4 + c))
                        last = project(1, tt, c, c == 0, c == 3)
                    last.then_inc(y_full, 1)
    return nc


_INS = ["x_prompt", "x_sample", "cache_k", "cache_v", "page_table", "g_pre", "w_in", "g_sgu",
        "w_spatial", "b_spatial", "w_out", "g_post"]
_OUTS = [(1, SEQ, D), (DEC_B, DEC_T, D), (1, 1, SEQ, KVH, HD), (1, 1, SEQ, KVH, HD),
         (1, DEC_B, DEC_T, KVH, HD), (1, DEC_B, DEC_T, KVH, HD), (1, DEC_B, DEC_T, GRP * GCH)]


def kernel(**inputs):
    import numpy as np
    import concourse.bacc as bacc
    from concourse.bass_utils import run_bass_kernel_spmd

    nc = bacc.Bacc("TRN2", target_bir_lowering=False, num_devices=1)
    arrays, args = {}, []
    for name in _INS:
        a = np.ascontiguousarray(inputs[name])
        arrays[f"in_{name}"] = a
        args.append(nc.dram_tensor(f"in_{name}", a.shape, mybir.dt.from_np(a.dtype), kind="ExternalInput").ap())
    for n, shape in enumerate(_OUTS):
        args.append(nc.dram_tensor(f"out_{n}", shape, fp32, kind="ExternalOutput").ap())
    build(nc, *args)
    r = run_bass_kernel_spmd(nc, [arrays], core_ids=[0])
    return tuple(r.results[0][f"out_{n}"] for n in range(len(_OUTS)))
```
